# Optimizing a Trainium2 kernel written in Bass

```python
import jax
import jax.numpy as jnp
from jax import lax
import numpy as np

D_MODEL = 1024
BATCH = 1
SEQ = 256
DEPTH = 1
DEC_BATCH = 8
DEC_SEQ = 8
PAST_LEN = 1024
PAGE_SIZE = 128

D_CONV = D_MODEL // 2
N_HEADS = 8
QK_NOPE_DIM = 64
QK_ROPE_DIM = 32
QK_DIM = QK_NOPE_DIM + QK_ROPE_DIM
V_DIM = 64
D_ATTN = N_HEADS * V_DIM
D_MIX = D_CONV + D_ATTN
Q_LORA_RANK = 3 * D_MODEL // 8
KV_LORA_RANK = D_MODEL // 4
D_IN = 2 * D_CONV + Q_LORA_RANK + KV_LORA_RANK + QK_ROPE_DIM
CONV_WIDTH = 31
N_EXPERTS = 32
TOP_K = 4
D_EXPERT = D_MODEL
SWIGLU_LIMIT = 7.0
SWIGLU_ALPHA = 1.702
ROPE_THETA = 10000.0
Q_BLOCK = 128
EXPERT_BLOCK = 128
NORM_EPS = 1e-6
ATTN_SCALE = QK_DIM ** -0.5

kernel_name = "hymba_conformer_mla_moe_step"

def _rmsnorm(x, g):
    xf = x.astype(jnp.float32)
    y = xf * lax.rsqrt(jnp.mean(xf * xf, axis=-1, keepdims=True) + NORM_EPS)
    return (y * g.astype(jnp.float32)).astype(x.dtype)

def _layernorm(x, g, b):
    xf = x.astype(jnp.float32)
    mu = jnp.mean(xf, axis=-1, keepdims=True)
    xc = xf - mu
    var = jnp.mean(xc * xc, axis=-1, keepdims=True)
    return (xc * lax.rsqrt(var + NORM_EPS) * g.astype(jnp.float32) + b.astype(jnp.float32)).astype(x.dtype)

def _rope_tables(pos):
    half = QK_ROPE_DIM // 2
    inv_freq = ROPE_THETA ** (-jnp.arange(half, dtype=jnp.float32) / half)
    ang = pos.astype(jnp.float32)[:, None] * inv_freq[None, :]
    return jnp.cos(ang), jnp.sin(ang)

def _rope(x, cos, sin):
    half = QK_ROPE_DIM // 2
    x1, x2 = x[..., :half], x[..., half:]
    cos = cos.astype(x.dtype)
    sin = sin.astype(x.dtype)
    return jnp.concatenate([x1 * cos - x2 * sin, x2 * cos + x1 * sin], axis=-1)

def _qk_norm(x, g_pairs):
    g_rot = g_pairs[QK_NOPE_DIM:]
    g = jnp.concatenate([g_pairs[:QK_NOPE_DIM], g_rot, g_rot])
    return _rmsnorm(x, g)

def _mixer_inputs(xn, pos, w_in, g_q_lat, w_uq, g_kv_lat, g_qk_q):
    proj = xn @ w_in
    a, gt, q_lat, kv_lat, k_rope = jnp.split(
        proj, [D_CONV, 2 * D_CONV, 2 * D_CONV + Q_LORA_RANK, 2 * D_CONV + Q_LORA_RANK + KV_LORA_RANK], axis=-1)
    glu = a * jax.nn.sigmoid(gt)
    cos, sin = _rope_tables(pos)
    q = jnp.einsum('btr,rhd->bthd', _rmsnorm(q_lat, g_q_lat), w_uq)
    q_rot = _rope(q[..., QK_NOPE_DIM:], cos[:, None, :], sin[:, None, :])
    q = _qk_norm(jnp.concatenate([q[..., :QK_NOPE_DIM], q_rot], axis=-1), g_qk_q)
    c_kv = _rmsnorm(kv_lat, g_kv_lat)
    k_rope = _rope(k_rope, cos, sin)
    return glu, q, c_kv, k_rope

def _latent_keys_values(c_kv, k_rope, w_ukv, g_qk_k):
    kv = jnp.einsum('...lc,chd->...lhd', c_kv, w_ukv)
    k_nope, v = kv[..., :QK_NOPE_DIM], kv[..., QK_NOPE_DIM:]
    k_r = jnp.broadcast_to(k_rope[..., None, :], k_nope.shape[:-1] + (QK_ROPE_DIM,))
    k = _qk_norm(jnp.concatenate([k_nope, k_r], axis=-1), g_qk_k)
    return k, v

def _attend(q, k, v, q_pos, k_pos):
    s = jnp.einsum('...qhd,...khd->...hqk', q, k).astype(jnp.float32) * ATTN_SCALE
    s = jnp.where(k_pos[None, :] <= q_pos[:, None], s, -jnp.inf)
    p = jax.nn.softmax(s, axis=-1).astype(v.dtype)
    return jnp.einsum('...hqk,...khd->...qhd', p, v)

def _mla_prompt(q, k, v):
    b, s = q.shape[0], q.shape[1]
    n_blk = s // Q_BLOCK
    q_blocks = q.reshape(b, n_blk, Q_BLOCK, N_HEADS, QK_DIM).swapaxes(0, 1)
    k_pos = jnp.arange(s)

    def one_block(args):
        qb, blk = args
        q_pos = blk * Q_BLOCK + jnp.arange(Q_BLOCK)
        return _attend(qb, k, v, q_pos, k_pos)

    o = lax.map(one_block, (q_blocks, jnp.arange(n_blk)))
    return o.swapaxes(0, 1).reshape(b, s, D_ATTN)

def _mla_sample(q, c_new, kr_new, page_table, cache_c, cache_kr, w_ukv, g_qk_k):
    n_past = page_table.shape[1] * PAGE_SIZE
    t = q.shape[1]
    q_pos = n_past + jnp.arange(t)
    k_pos = jnp.arange(n_past + t)

    def one_seq(args):
        pages, qs, cn, krn = args
        c = jnp.concatenate([cache_c[pages].reshape(n_past, KV_LORA_RANK), cn], axis=0)
        kr = jnp.concatenate([cache_kr[pages].reshape(n_past, QK_ROPE_DIM), krn], axis=0)
        k, v = _latent_keys_values(c, kr, w_ukv, g_qk_k)
        return _attend(qs, k, v, q_pos, k_pos)

    o = lax.map(one_seq, (page_table, q, c_new, kr_new))
    return o.reshape(q.shape[0], t, D_ATTN)

def _conv_module(buf, conv_w, conv_b, ln_g, ln_b):
    y = lax.conv_general_dilated(buf, conv_w[:, None, :], window_strides=(1,), padding='VALID',
                                 dimension_numbers=('NWC', 'WIO', 'NWC'),
                                 feature_group_count=D_CONV) + conv_b
    return jax.nn.silu(_layernorm(y, ln_g, ln_b))

def _merge(conv_out, attn_out, g_out_conv, g_out_attn, w_out):
    y = jnp.concatenate([_rmsnorm(conv_out, g_out_conv), _rmsnorm(attn_out, g_out_attn)], axis=-1)
    return y @ w_out

def _moe(xt, w_router, b_router, w_gate_up, b_gate_up, w_down, b_down):
    n_tok = xt.shape[0]
    n_assign = n_tok * TOP_K
    logits = (xt @ w_router).astype(jnp.float32) + b_router.astype(jnp.float32)
    top_logit, top_expert = lax.top_k(logits, TOP_K)
    gates = jax.nn.softmax(top_logit, axis=-1)
    flat_expert = top_expert.reshape(-1)
    order = jnp.argsort(flat_expert)
    sorted_expert = flat_expert[order]
    counts = jnp.bincount(flat_expert, length=N_EXPERTS)
    padded = (counts + EXPERT_BLOCK - 1) // EXPERT_BLOCK * EXPERT_BLOCK
    start_sorted = jnp.cumsum(counts) - counts
    padded_end = jnp.cumsum(padded)
    start_padded = padded_end - padded
    slot = start_padded[sorted_expert] + jnp.arange(n_assign) - start_sorted[sorted_expert]
    n_blocks = -(-n_assign // EXPERT_BLOCK) + N_EXPERTS
    x_slots = jnp.zeros((n_blocks * EXPERT_BLOCK, D_MODEL), xt.dtype).at[slot].set(xt[order // TOP_K])
    block_expert = jnp.minimum(
        jnp.searchsorted(padded_end, jnp.arange(n_blocks) * EXPERT_BLOCK, side='right'), N_EXPERTS - 1)

    def expert_block(args):
        xb, e = args
        gu = xb @ w_gate_up[e] + b_gate_up[e]
        gate = jnp.minimum(gu[:, :D_EXPERT], SWIGLU_LIMIT)
        up = jnp.clip(gu[:, D_EXPERT:], -SWIGLU_LIMIT, SWIGLU_LIMIT)
        h = (up + 1.0) * gate * jax.nn.sigmoid(SWIGLU_ALPHA * gate)
        return h @ w_down[e] + b_down[e]

    y_slots = lax.map(expert_block, (x_slots.reshape(n_blocks, EXPERT_BLOCK, D_MODEL), block_expert))
    y_slots = y_slots.reshape(n_blocks * EXPERT_BLOCK, D_MODEL)
    y_assign = jnp.zeros((n_assign, D_MODEL), xt.dtype).at[order].set(y_slots[slot])
    return jnp.einsum('tkd,tk->td', y_assign.reshape(n_tok, TOP_K, D_MODEL), gates.astype(xt.dtype))

def setup_inputs(seed: int = 0) -> dict:
    key = jax.random.key(seed)
    ks = jax.random.split(key, 32)
    f32 = jnp.float32
    n_pages = PAST_LEN // PAGE_SIZE
    n_used = DEC_BATCH * n_pages
    n_pool = n_used + n_used // 4 + 1

    def normal(k, shape, scale):
        return scale * jax.random.normal(k, shape, f32)

    def gain(k, n):
        return 1.0 + normal(k, (DEPTH, n), 0.1)

    page_table = jax.random.permutation(ks[5], n_pool)[:n_used].reshape(DEC_BATCH, n_pages).astype(jnp.int32)
    return {
        "x_prompt": normal(ks[0], (BATCH, SEQ, D_MODEL), 1.0),
        "x_sample": normal(ks[1], (DEC_BATCH, DEC_SEQ, D_MODEL), 1.0),
        "cache_kv_latent": normal(ks[2], (DEPTH, n_pool, PAGE_SIZE, KV_LORA_RANK), 1.0),
        "cache_k_rope": normal(ks[3], (DEPTH, n_pool, PAGE_SIZE, QK_ROPE_DIM), 1.0),
        "state_conv": normal(ks[4], (DEPTH, DEC_BATCH, CONV_WIDTH - 1, D_CONV), 0.5),
        "page_table": page_table,
        "norm_mix": gain(ks[6], D_MODEL),
        "w_in": normal(ks[7], (DEPTH, D_MODEL, D_IN), D_MODEL ** -0.5),
        "norm_q_lat": gain(ks[8], Q_LORA_RANK),
        "w_uq": normal(ks[9], (DEPTH, Q_LORA_RANK, N_HEADS, QK_DIM), Q_LORA_RANK ** -0.5),
        "norm_kv_lat": gain(ks[10], KV_LORA_RANK),
        "w_ukv": normal(ks[11], (DEPTH, KV_LORA_RANK, N_HEADS, QK_NOPE_DIM + V_DIM), KV_LORA_RANK ** -0.5),
        "norm_qk_q": gain(ks[12], QK_NOPE_DIM + QK_ROPE_DIM // 2),
        "norm_qk_k": gain(ks[13], QK_NOPE_DIM + QK_ROPE_DIM // 2),
        "conv_w": normal(ks[14], (DEPTH, CONV_WIDTH, D_CONV), CONV_WIDTH ** -0.5),
        "conv_b": normal(ks[15], (DEPTH, D_CONV), 0.01),
        "conv_ln_g": gain(ks[16], D_CONV),
        "conv_ln_b": normal(ks[17], (DEPTH, D_CONV), 0.01),
        "norm_out_conv": gain(ks[18], D_CONV),
        "norm_out_attn": gain(ks[19], D_ATTN),
        "w_out": normal(ks[20], (DEPTH, D_MIX, D_MODEL), D_MIX ** -0.5),
        "norm_ffn": gain(ks[21], D_MODEL),
        "w_router": normal(ks[22], (DEPTH, D_MODEL, N_EXPERTS), D_MODEL ** -0.5),
        "b_router": normal(ks[23], (DEPTH, N_EXPERTS), 0.01),
        "w_gate_up": normal(ks[24], (DEPTH, N_EXPERTS, D_MODEL, 2 * D_EXPERT), D_MODEL ** -0.5),
        "b_gate_up": normal(ks[25], (DEPTH, N_EXPERTS, 2 * D_EXPERT), 0.01),
        "w_down": normal(ks[26], (DEPTH, N_EXPERTS, D_EXPERT, D_MODEL), D_EXPERT ** -0.5),
        "b_down": normal(ks[27], (DEPTH, N_EXPERTS, D_MODEL), 0.01),
    }

def reference(x_prompt, x_sample, cache_kv_latent, cache_k_rope, state_conv, page_table,
              norm_mix, w_in, norm_q_lat, w_uq, norm_kv_lat, w_ukv, norm_qk_q, norm_qk_k,
              conv_w, conv_b, conv_ln_g, conv_ln_b, norm_out_conv, norm_out_attn, w_out,
              norm_ffn, w_router, b_router, w_gate_up, b_gate_up, w_down, b_down):
    pos_prompt = jnp.arange(x_prompt.shape[1])
    pos_sample = page_table.shape[1] * PAGE_SIZE + jnp.arange(x_sample.shape[1])
    h_p, h_s = x_prompt, x_sample
    lat_p, rope_p, conv_p, lat_s, rope_s, conv_s = [], [], [], [], [], []
    for l in range(DEPTH):
        glu_p, q_p, c_p, kr_p = _mixer_inputs(_rmsnorm(h_p, norm_mix[l]), pos_prompt, w_in[l],
                                              norm_q_lat[l], w_uq[l], norm_kv_lat[l], norm_qk_q[l])
        glu_s, q_s, c_s, kr_s = _mixer_inputs(_rmsnorm(h_s, norm_mix[l]), pos_sample, w_in[l],
                                              norm_q_lat[l], w_uq[l], norm_kv_lat[l], norm_qk_q[l])
        buf_p = jnp.concatenate(
            [jnp.zeros((glu_p.shape[0], CONV_WIDTH - 1, D_CONV), glu_p.dtype), glu_p], axis=1)
        buf_s = jnp.concatenate([state_conv[l].astype(glu_s.dtype), glu_s], axis=1)
        cv_p = _conv_module(buf_p, conv_w[l], conv_b[l], conv_ln_g[l], conv_ln_b[l])
        cv_s = _conv_module(buf_s, conv_w[l], conv_b[l], conv_ln_g[l], conv_ln_b[l])
        k_p, v_p = _latent_keys_values(c_p, kr_p, w_ukv[l], norm_qk_k[l])
        at_p = _mla_prompt(q_p, k_p, v_p)
        at_s = _mla_sample(q_s, c_s, kr_s, page_table, cache_kv_latent[l], cache_k_rope[l],
                           w_ukv[l], norm_qk_k[l])
        h_p = h_p + _merge(cv_p, at_p, norm_out_conv[l], norm_out_attn[l], w_out[l])
        h_s = h_s + _merge(cv_s, at_s, norm_out_conv[l], norm_out_attn[l], w_out[l])
        lat_p.append(c_p)
        rope_p.append(kr_p)
        conv_p.append(buf_p[:, -(CONV_WIDTH - 1):])
        lat_s.append(c_s)
        rope_s.append(kr_s)
        conv_s.append(buf_s[:, -(CONV_WIDTH - 1):])
        xn_p = _rmsnorm(h_p, norm_ffn[l])
        xn_s = _rmsnorm(h_s, norm_ffn[l])
        n_p = xn_p.shape[0] * xn_p.shape[1]
        xt = jnp.concatenate([xn_p.reshape(-1, D_MODEL), xn_s.reshape(-1, D_MODEL)], axis=0)
        yt = _moe(xt, w_router[l], b_router[l], w_gate_up[l], b_gate_up[l], w_down[l], b_down[l])
        h_p = h_p + yt[:n_p].reshape(h_p.shape)
        h_s = h_s + yt[n_p:].reshape(h_s.shape)
    prompt_kv_latent = jnp.stack(lat_p)
    prompt_k_rope = jnp.stack(rope_p)
    prompt_conv_state = jnp.stack(conv_p)
    sample_kv_latent = jnp.stack(lat_s)
    sample_k_rope = jnp.stack(rope_s)
    sample_conv_state = jnp.stack(conv_s)
    return (h_p, h_s, prompt_kv_latent, prompt_k_rope, prompt_conv_state,
            sample_kv_latent, sample_k_rope, sample_conv_state)


_drawn_inputs = setup_inputs


def setup_inputs(seed=0):
    import zlib

    import numpy as np

    out = dict(_drawn_inputs(seed))
    spreads = {}
    factors = {'b_gate_up': 8.0, 'b_down': 8.0}
    for name, (base, spread) in spreads.items():
        noise = np.random.default_rng([zlib.crc32(name.encode()), seed]).standard_normal(out[name].shape)
        drawn = base * np.exp(spread * noise) if base else spread * noise
        out[name] = jnp.asarray(drawn.astype(out[name].dtype))
    for name, factor in factors.items():
        out[name] = (out[name] * factor).astype(out[name].dtype)
    return out
```

```python
import concourse.bass as bass
from concourse import mybir
from concourse.alu_op_type import AluOpType as ALU
from contextlib import ExitStack

F32 = mybir.dt.float32
I32 = mybir.dt.int32
U32 = mybir.dt.uint32
ACT = mybir.ActivationFunctionType
X_AXIS = mybir.AxisListType.X

D = 1024
KD = D // 128
SEQ, DEC_B, DEC_T = 256, 8, 8
NS = DEC_B * DEC_T
T = SEQ + NS
CHUNKS = [(0, 128), (128, 128), (256, NS)]
ORDER = (2, 0, 1)
NC = len(CHUNKS)
DC = 512
CC = DC // 128
W = 31
H, DN, DR, DV = 8, 64, 32, 64
DQ = DN + DR
QL, KVL = 384, 256
D_IN = 2 * DC + QL + KVL + DR
PAGE, PAGES = 128, 8
POOL_PAGES = 81
NE, TOPK = 32, 4
DE = 1024
LIMIT, ALPHA = 7.0, 1.702
EPS = 1e-6
SCALE = DQ ** -0.5
BIG = 4096.0
SLOTS = 64
OVER = 20
OVER_W = 64
ITEMS = NE + OVER_W
MAX_ITER = (NE + OVER) // 2

ONE, LAT = DR, DR + 4
CROW = LAT + KVL
SEG = W + DEC_T
SEG0 = W - 1 + SEQ
GLU_W = SEG0 + DEC_B * SEG
C_ID, C_UP, C_ONE, C_CAUS, C_IOTA, C_PIDX, C_EPS, C_ONE0 = 0, 128, 256, 384, 768, 832, 833, 834
C_W = 834 + 64


def decoder_layer(nc, ins, consts, outs):
    (x_prompt, x_sample, cache_kv, cache_kr, state_conv, page_table, norm_mix, w_in, norm_q_lat,
     w_uq, norm_kv_lat, w_ukv, norm_qk_q, norm_qk_k, conv_w, conv_b, conv_ln_g, conv_ln_b,
     norm_out_conv, norm_out_attn, w_out, norm_ffn, w_router, b_router, w_gate_up, b_gate_up,
     w_down, b_down) = ins
    c_pack, c_cos, c_sin = consts
    y_p, y_s, lat_p, rope_p, conv_p, lat_s, rope_s, conv_s = outs

    ctx = ExitStack()
    with ctx:
        arena_w = 16384 + 8192 + 3072 + 13568 + 8544
        sb = ctx.enter_context(nc.sbuf_tensor("arena", [128, arena_w], F32))

        def view(off, *dims, rows=128):
            n = 1
            for d in dims:
                n *= d
            v = sb[0:rows, off:off + n]
            if len(dims) == 2:
                v = v.rearrange("p (a b) -> p a b", a=dims[0])
            if len(dims) == 3:
                v = v.rearrange("p (a b c) -> p a b c", a=dims[0], b=dims[1])
            return v

        def own(name, shape, dt=F32):
            return ctx.enter_context(nc.sbuf_tensor(name, shape, dt))

        R_GU, R_DN = 0, 16384
        R_X = R_DN + 8192
        R_W = R_X + 3072
        R_M = R_W + 13568
        gu_ring = view(R_GU, KD, 2 * DE)
        dn_ring = view(R_DN, KD, D)
        X = view(R_X, NC, D)
        o = R_GU

        def take(n):
            nonlocal o
            o += n
            return o - n
        ql = view(take(NC * QL), NC, QL)
        ckvT = view(take(2 * T), 2, T)
        qlT = view(take(3 * T), 3, T)
        s_prod = view(o, 64, W)
        eg = view(take(2 * T), 2, T)
        sqs = view(take(2 * 768), 2, 768)
        qsn = view(take(512), 512)
        qsr = view(take(352), 352)
        qsT = view(take(4 * 128), 4, 2 * NS)
        snew = view(take(512), 512)
        wkT = view(take(4 * KVL), 4, KVL)
        R_U = take(2304)
        wuq = view(R_U, 3, 768)
        s_all = [view(R_U + 512 * i, PAGES, 64) for i in range(2)]
        sqk = [view(R_U + 1024 + 512 * i, 512) for i in range(2)]
        pr = [view(R_U + 384 * i, 3, 128) for i in range(2)]
        pT = [view(R_U + 768 + 384 * i, 3, 128) for i in range(2)]
        qt = [view(o + 768 * i, 768) for i in range(3)]
        st_rows = view(take(2 * DC), 2, DC)[0:120]
        rows1 = view(take(128), 128)[0:W * CC]
        rows2 = view(take(128), 128)[0:31]
        row_out = view(take(DC), DC)[0:NS]
        row_out2 = view(take(DC), DC)[0:32]
        gpk = view(take(CC * NS), CC, NS)
        sqr = view(take(PAGES * DR), PAGES, DR)
        ocn = view(take(KVL), KVL)
        gkv = view(take(KVL), KVL)
        gqk = view(take(DQ), DQ)
        gkk = view(take(DQ), DQ)
        cos = view(take(NC * 16), NC, 16)
        sin = view(take(NC * 16), NC, 16)
        rope_a = view(take(128), 128)
        rope_b = view(take(128), 128)
        ckv = view(take(NC * CROW), NC, CROW)
        assert o <= R_DN, o
        o = R_DN
        qT = view(take(H * SEQ), H, SEQ)
        kT = view(take(H * SEQ), H, SEQ)
        vt = view(take(2 * 576), 2, 576)
        qabs = view(take(2 * 512), 2, 512)
        kt = [view(o + 768 * i, 768) for i in range(2)]
        ocT = view(take(2 * 512), 2, 512)
        cT = view(take(2 * 384), 2, 384)
        assert o <= R_X
        win = view(R_W, KD, D_IN)
        wout = view(R_W, KD, D)
        ck = [view(R_W + 8192 + i * PAGES * CROW, PAGES, CROW) for i in range(2)]
        lng = view(R_W + 8192, DC)
        lnb = view(R_W + 8192 + 512, DC)
        conv_t = view(R_W + 8192 + 1024, NC, DC)
        attn_t = view(R_W + 8192 + 2560, NC, DC)
        assert 8192 + 2560 + 1536 <= 13568
        o = R_W
        xn2 = view(take(NC * D), NC, D)
        xg = view(take(KD * 128), KD, 128)
        ysb = view(take(2 * 512), 2, 512)
        sel = view(take(NC * 128), NC, 128)
        selg = view(take(NC * 192), NC, 192)
        selT = view(take(2 * NC * 128), 2, NC * 128)
        posI = view(take(NC * ITEMS), NC, ITEMS)
        gateI = view(take(NC * ITEMS), NC, ITEMS)
        bias = [view(take(2 * DE), 2 * DE) for _ in range(2)]
        assert o <= R_M
        o = R_M
        xT = view(take(KD * T), KD, T)
        wk = view(take(2 * 512), 2, 512)
        wv = view(take(2 * 512), 2, 512)
        R_C = take(CC * GLU_W)
        glu = view(R_C, CC, GLU_W)
        acc = view(take(CC * 384), CC, 384)
        xn = view(R_C, NC, D)
        gsb = [view(R_C + 512 * i, 512) for i in range(5)]
        bdn = view(R_M + KD * T, D)
        assert take(0) - R_M <= 8544, take(0) - R_M
        o = R_C + 3 * 512
        lgT = view(take(384), 384)[0:NE]
        GT = view(take(384), 384)
        posT = view(take(384), 384)[0:NE]
        extra = view(take(128), 128)[0:NE]
        rel, tmpP, P = (view(take(64), 64)[0:NE] for _ in range(3))
        lg, M, G, eq = (view(take(NC * NE), NC, NE) for _ in range(4))
        assert o <= R_M + 8544, o

        cst = own("cst", [128, C_W])
        ident = cst[:, C_ID:C_ID + 128]
        upper = cst[:, C_UP:C_UP + 128]
        ones = cst[:, C_ONE:C_ONE + 128]
        causal3 = cst[:, C_CAUS:C_CAUS + 384]
        iota = cst[:, C_IOTA:C_IOTA + 64]
        pidx = cst[:, C_PIDX:C_PIDX + 1]
        eps = cst[:, C_EPS:C_EPS + 1]
        one_row = cst[:, C_ONE0:C_ONE0 + 64]
        cw = own("cw", [128, 32 * CC])
        gc = own("gc", [128, 31])
        g_mix, g_ql, g_cb, g_oc, g_oa, g_ffn = (gc[:, a:b] for a, b in
                                                ((0, 8), (8, 11), (11, 15), (15, 19), (19, 23), (23, 31)))
        ss = own("ss", [128, 16])
        rs = own("rs", [128, 16])
        lnx = own("lnx", [128, 64])
        s8 = own("s8", [128, PAGES, H])
        r8 = own("r8", [128, PAGES, H])
        rss = own("rss", [128, PAGES])
        m1 = own("m1", [128, 128])
        mx = own("mx", [128, 2])
        dg = own("dg", [128, 128])
        pn = own("pn", [128, 64])
        rden = own("rden", [128, 2])
        pt_sb = own("pt_sb", [1, DEC_B * PAGES], I32)
        qrT = own("qrT", [128, 512])
        krn = own("krn", [128, NS])
        pm = own("pm", [128, 2, 2])
        psm = own("psm", [128, 2, 2])
        rsm = own("rsm", [128, 2, 2])
        wr = own("wr", [128, KD, NE])
        br = own("br", [128, NE])
        v8 = own("v8", [128, NC, 8])
        i8 = own("i8", [128, NC, 8], U32)
        i8f = own("i8f", [128, NC, 8])
        gate4 = own("gate4", [128, NC, TOPK])
        gsum = own("gsum", [128, NC])
        tab_f = own("tab_f", [1, 80])
        tab = own("tab", [1, 80], I32)
        st6 = own("st6", [128, 6])
        mv = own("mv", [128, NC, 2])

        PS = [ctx.enter_context(nc.psum_tensor(f"bank{i}", [128, 512], F32)) for i in range(8)]

        sems = {}

        def S(name):
            if name not in sems:
                sems[name] = ctx.enter_context(nc.semaphore(name))
            return sems[name]

        def bc(ap, shape, axis):
            return ap.unsqueeze(axis).broadcast_to(shape)

        def page_count(n, t):
            return (n - t) * (8 * PAGES) + 16 * PAGES

        def windows(c):
            v = glu[:, bass.ds(c, 1), SEG0:GLU_W].rearrange("p c (s u) -> p (c s) u", u=SEG)[:, :, 0:DEC_T]
            return bass.AP(v.tensor, v.offset, [list(d) for d in v.ap] + [[1, W]])

        block = ctx.enter_context(nc.Block())

        @block.sync
        def _(sp):
            sp.dma_start(X[:, 0:2, :], x_prompt[0].rearrange("(c p) d -> p c d", p=128)).then_inc(S("x_in"), 16)
            sp.dma_start(X[0:NS, 2, :], x_sample.rearrange("b t d -> (b t) d")).then_inc(S("x_in"), 16)
            sp.wait_ge(S("g_in"), 80)
            sp.wait_ge(S("st_in"), 32)
            for cols, arrived in ((slice(2 * DC, D_IN), "win_in"), (slice(0, 2 * DC), "winc_in")):
                for kk in range(2):
                    sp.dma_start(win[:, 4 * kk:4 * kk + 4, cols],
                                 w_in[0, 512 * kk:512 * kk + 512, cols].rearrange("(k p) n -> p k n", p=128)).then_inc(S(arrived), 16)
            w4 = w_ukv[0].rearrange("(l p) h d -> l p h d", p=128)
            for l in range(2):
                sp.dma_start(wk[:, l, :].rearrange("p (h d) -> p h d", h=H), w4[l][:, :, 0:DN]).then_inc(S("wkv_in"), 16)
                sp.dma_start(wv[:, l, :].rearrange("p (h d) -> p h d", h=H), w4[l][:, :, DN:128]).then_inc(S("wkv_in"), 16)
            sp.dma_start(wuq, w_uq[0].rearrange("(k p) h d -> p k (h d)", p=128)).then_inc(S("wuq_in"), 16)

            def load_pages(n, t, first):
                pages = [sp.value_load(pt_sb[0:1, bass.ds(n * PAGES + j, 1)], min_val=0, max_val=POOL_PAGES - 1)
                         for j in range(PAGES)]
                if not first:
                    sp.wait_ge(S("ck_used"), n - 1)
                for j, page in enumerate(pages):
                    arrived = S(f"ck_in{t}" if j < PAGES // 2 else f"ck2_in{t}")
                    sp.dma_start(ck[t][:, j, LAT:CROW],
                                 cache_kv[0, bass.ds(page, 1)].rearrange("a p c -> p (a c)")).then_inc(arrived, 16)
                    sp.dma_start(ck[t][:, j, 0:DR],
                                 cache_kr[0, bass.ds(page, 1)].rearrange("a p c -> p (a c)")).then_inc(arrived, 16)

            sp.wait_ge(S("pt_in"), 16)
            sp.wait_ge(S("proj_done"), 3 + 2 * CC)
            load_pages(0, 0, True)
            load_pages(1, 1, True)
            sp.dma_start(wout, w_out[0].rearrange("(k p) n -> p k n", p=128)).then_inc(S("wout_in"), 16)

            def gu_slot(e, j):
                sp.dma_start(gu_ring[:, 2 * j:2 * j + 2, :],
                             w_gate_up[0, bass.ds(e, 1), 256 * j:256 * j + 256]
                             .rearrange("a (k p) n -> p k (a n)", p=128)).then_inc(S(f"gu_in{j}"), 16)

            def dn_slot(e, j):
                sp.dma_start(dn_ring[:, 4 * j:4 * j + 4, :],
                             w_down[0, bass.ds(e, 1), 512 * j:512 * j + 512]
                             .rearrange("a (k p) n -> p k (a n)", p=128)).then_inc(S(f"dn_in{j}"), 16)

            def bias_row(e, t):
                sp.dma_start(bias[t][0:1, :], b_gate_up[0, bass.ds(e, 1), :]).then_inc(S(f"bias_in{t}"), 16)

            with sp.Fori(1, 4) as i:
                load_pages(2 * i, 0, False)
                load_pages(2 * i + 1, 1, False)
            sp.wait_ge(S("ck_used"), DEC_B)
            sp.dma_start(lng, conv_ln_g[0:1].partition_broadcast(128)).then_inc(S("ln_in"), 16)
            sp.dma_start(lnb, conv_ln_b[0:1].partition_broadcast(128)).then_inc(S("ln_in"), 16)

            sp.wait_ge(S("attn_done"), 1)
            sp.wait_ge(S("out"), 16 * 14)
            for j in range(4):
                gu_slot(0, j)
            dn_slot(0, 0)
            dn_slot(0, 1)
            sp.wait_ge(S("moe_zero"), 1)
            bias_row(0, 0)

            def item(n, e, t):
                if isinstance(n, int) and n < 2:
                    pass
                else:
                    sp.wait_ge(S(f"bias_used{t}"), (n - t) // 2 if isinstance(n, int) else n_half[0])
                bias_row(e, t)
                for j in range(4):
                    sp.wait_ge(S(f"gu_used{j}" if j < 3 else "gu_done"), n)
                    gu_slot(e, j)
                for j in range(2):
                    sp.wait_ge(S("dn_used0" if j == 0 else "dn_done"), n)
                    dn_slot(e, j)
            n_half = [None]
            item(1, 1, 1)
            with sp.Fori(1, NE // 2) as i:
                n_half[0] = i
                item(2 * i, 2 * i, 0)
                item(2 * i + 1, 2 * i + 1, 1)
            sp.wait_ge(S("table"), 1)
            n_iter = sp.value_load(tab[0:1, 0:1], min_val=NE // 2, max_val=MAX_ITER)
            with sp.If(n_iter > NE // 2):
                with sp.Fori(NE // 2, n_iter) as i:
                    n_half[0] = i
                    for t in range(2):
                        e = sp.value_load(tab[0:1, bass.ds(2 * i + (t + 1 - NE), 1)], min_val=0, max_val=NE - 1)
                        item(2 * i + t, e, t)
                sp.nop()
            sp.wait_ge(S("y_done"), 1)
            sp.dma_start(y_p[0].rearrange("(c p) d -> p c d", p=128), X[:, 0:2, :]).then_inc(S("y_out"), 16)
            sp.dma_start(y_s.rearrange("b t d -> (b t) d"), X[0:NS, 2, :]).then_inc(S("y_out"), 16)
            sp.wait_ge(S("y_out"), 32)

        @block.gpsimd
        def _(pool):
            pool.dma_start(pt_sb[:], page_table.rearrange("(a b) p -> a (b p)", a=1)).then_inc(S("pt_in"), 16)
            for t in (ss, rs):
                pool.memset(t[:], 0.0)
            pool.memset(cw[:, W * CC:32 * CC], 0.0).then_inc(S("zeroed"), 1)
            for t in (m1, dg, pn, qrT):
                pool.memset(t[:], 0.0)
            pool.memset(ckv[:], 0.0)
            pool.drain()
            pool.memset(X[NS:128, 2, :], 0.0)
            pool.drain()
            pool.memset(qsr, 0.0)
            pool.memset(ocn, 0.0)
            pool.memset(qsT, 0.0)
            pool.memset(vt[:, :, 512:576], 0.0).then_inc(S("zeroed"), 1)
            pool.wait_ge(S("zeroed"), 2)
            pool.drain()
            pool.drain()
            pool.memset(ckv[0:NS, 2, ONE:LAT], 1.0)
            pool.drain()
            pool.memset(ckv[:, 0:2, ONE:LAT], 1.0).then_inc(S("zeroed"), 1)
            pool.dma_start(wr[:], w_router[0].rearrange("(k p) e -> p k e", p=128)).then_inc(S("wr_in"), 16)
            pool.dma_start(br[:], b_router[0:1].partition_broadcast(128)).then_inc(S("wr_in"), 16)
            pool.dma_start(conv_s[0, :, 0:W - 1 - DEC_T, :], state_conv[0, :, DEC_T:W - 1, :]).then_inc(S("out"), 16)
            pool.wait_ge(S("x_T"), 6)
            pool.memset(glu[:, :, 0:W - 1], 0.0)
            pool.memset(glu[:, :, SEG0:GLU_W].rearrange("p c (s u) -> p c s u", u=SEG)[:, :, :, SEG - 1:SEG], 0.0)
            pool.memset(acc, 0.0).then_inc(S("conv_zero"), 1)
            pool.wait_ge(S("proj_done"), 3 + 2 * CC)
            pool.memset(ck[0][:, :, ONE:LAT], 1.0)
            pool.memset(ck[1][:, :, ONE:LAT], 1.0).then_inc(S("ck_ones"), 1)
            pool.wait_ge(S("ckv_done"), 3)
            pool.dma_start(lat_p[0, 0].rearrange("(c p) d -> p c d", p=128), ckv[:, 0:2, LAT:CROW]).then_inc(S("out"), 16)
            pool.dma_start(rope_p[0, 0].rearrange("(c p) d -> p c d", p=128), ckv[:, 0:2, 0:DR]).then_inc(S("out"), 16)
            pool.dma_start(lat_s[0].rearrange("b t d -> (b t) d"), ckv[0:NS, 2, LAT:CROW]).then_inc(S("out"), 16)
            pool.dma_start(rope_s[0].rearrange("b t d -> (b t) d"), ckv[0:NS, 2, 0:DR]).then_inc(S("out"), 16)
            pool.wait_ge(S("snew"), 1)
            v = snew[0:NS].rearrange("p (s h q) -> p s h q", s=8, h=8)
            pool.affine_select(out=v, in_=v, compare_op=ALU.is_ge, fill=-1e30, base=0,
                               pattern=[[-8, 8], [0, 8], [0, 8]], channel_multiplier=1).then_inc(S("snew_m"), 1)
            pool.wait_ge(S("snew_m"), 1)
            pool.affine_select(out=v, in_=v, compare_op=ALU.is_ge, fill=-1e30, base=0,
                               pattern=[[8, 8], [0, 8], [1, 8]], channel_multiplier=-1).then_inc(S("snew_m"), 1)
            def rope_squares(n, t, first):
                pool.wait_ge(S(f"ck_in{t}"), page_count(n, t))
                pool.wait_ge(S(f"ck2_in{t}"), page_count(n, t))
                if not first:
                    pool.wait_ge(S("rss_done"), n)
                pool.tensor_tensor(sqr[:], ck[t][:, :, 0:DR], ck[t][:, :, 0:DR], ALU.mult).then_inc(S("sqr"), 1)
            rope_squares(0, 0, True)
            pool.wait_ge(S("q_ss"), NC)
            pool.wait_ge(S("k_ss"), NC)
            pool.wait_ge(S("glu"), CC)

            def tap_products(c):
                pool.tensor_tensor(s_prod.rearrange("p (s q) j -> p s q j", s=DEC_B), windows(c),
                                   cw[:, 0:W * CC].rearrange("p (j c) -> p c j", c=CC)[:, bass.ds(c, 1), :].unsqueeze(1)
                                   .broadcast_to([128, DEC_B, DEC_T, W]), ALU.mult).then_inc(S("s_prod"), 1)
            tap_products(0)
            pool.wait_ge(S("rows_ev"), 1)
            for b in range(DEC_B):
                pool.dma_start(conv_s[0, b, W - 1 - DEC_T:W - 1, :], row_out[8 * b:8 * b + 8, :]).then_inc(S("out"), 16)
            pool.dma_start(conv_p[0, 0], row_out2[0:W - 1, :]).then_inc(S("out"), 16)
            with pool.Fori(0, 3) as i:
                rope_squares(2 * i + 1, 1, False)
                pool.wait_ge(S("s_sum"), i + 1)
                tap_products(i + 1)
                rope_squares(2 * i + 2, 0, False)
            rope_squares(7, 1, False)
            pool.wait_ge(S("merged"), 6)
            pool.memset(bdn, 0.0)
            pool.memset(lgT[:], 0.0)
            pool.memset(GT[:], 0.0)
            pool.drain()
            pool.memset(xn2[NS:128, 2, :], 0.0)
            pool.drain()
            pool.memset(ysb, 0.0).then_inc(S("y_ev"), 2)
            pool.memset(selT, 0.0).then_inc(S("selT"), 1)
            pool.memset(bias[0], 0.0)
            pool.memset(bias[1], 0.0).then_inc(S("moe_zero"), 1)
            pool.wait_ge(S("moe_zero"), 1)
            pool.dma_start(bdn[0:NE, :], b_down[0]).then_inc(S("bdn_in"), 16)

        @block.tensor
        def _(pe):
            def mm(out, lhsT, rhs, a, b):
                return pe.matmul(out, lhsT, rhs, start=a, stop=b)

            def tr(out, in_, n=128):
                return pe.transpose(out, in_, ident[0:n, 0:n])

            pe.wait_ge(S("cst_in"), 16)
            pe.wait_ge(S("rows_in"), 16 * 7)
            tr(PS[7][:, 0:124], rows1[:], 124)
            tr(PS[7][:, 128:159], rows2[:], 31).then_inc(S("gains_T"), 1)
            for g in range(6):
                c, n = g // 2, CHUNKS[g // 2][1]
                pe.wait_ge(S("xn"), c + 1)
                for j in range(4):
                    k = 4 * (g % 2) + j
                    last = tr(PS[g][:, 128 * j:128 * j + n], xn[0:n, c, 128 * k:128 * k + 128], n)
                last.then_inc(S("x_T"), 1)
            pe.wait_ge(S("st_in"), 32)
            pe.wait_ge(S("gains"), 1)
            for c in range(CC):
                for i in range(2):
                    last = tr(PS[6 + c // 2][:, 256 * (c % 2) + 120 * i:256 * (c % 2) + 120 * i + 120],
                              st_rows[:, i, 128 * c:128 * c + 128], 120)
            last.then_inc(S("state_T"), 1)
            pe.wait_ge(S("win_in"), 32)
            pe.wait_ge(S("xT"), 6)
            for c in ORDER:
                r, n = CHUNKS[c]
                for k in range(KD):
                    mm(PS[2 * c][0:n, 0:QL], xT[:, k, r:r + n], win[:, k, 1024:1408], k == 0, k == KD - 1)
                for k in range(KD):
                    last = mm(PS[2 * c + 1][0:n, 0:288], xT[:, k, r:r + n], win[:, k, 1408:1696], k == 0, k == KD - 1)
                last.then_inc(S("proj_done"), 1)

            def conv_in(c):
                a, g = (PS[6], PS[7]) if c % 2 == 0 else (PS[0], PS[1])
                if c == 0:
                    pe.wait_ge(S("state_ev"), CC)
                    pe.wait_ge(S("winc_in"), 32)
                if c == 1:
                    pe.wait_ge(S("ckv_done"), 2)
                if c >= 2:
                    pe.wait_ge(S("glu"), c - 1)
                for k in range(KD):
                    last = mm(g[:, 0:T], win[:, k, DC + 128 * c:DC + 128 * c + 128], xT[:, k, :], k == 0, k == KD - 1)
                last.then_inc(S("proj_done"), 1)
                for k in range(KD):
                    last = mm(a[:, 0:T], win[:, k, 128 * c:128 * c + 128], xT[:, k, :], k == 0, k == KD - 1)
                last.then_inc(S("proj_done"), 1)

            def q_up(i):
                r, n = CHUNKS[ORDER[i]]
                if i == 0:
                    pe.wait_ge(S("wuq_in"), 16)
                    pe.wait_ge(S("qlT"), 3)
                else:
                    pe.wait_ge(S("q_rope"), i)
                for hb in range(2):
                    for j in range(3):
                        last = mm(PS[4 + hb][0:n, 0:384], qlT[:, j, r:r + n], wuq[:, j, 384 * hb:384 * hb + 384], j == 0, j == 2)
                last.then_inc(S("q_up"), 1)

            def kv_up(i):
                r, n = CHUNKS[ORDER[i]]
                if i:
                    pe.wait_ge(S("glu"), 2 + i)
                for b, w in (((2, wk),), ((6, wk), (7, wv)), ((0, wk), (1, wv)))[i]:
                    for l in range(2):
                        last = mm(PS[b][0:n, 0:512], ckvT[:, l, r:r + n], w[:, l, :], l == 0, l == 1)
                last.then_inc(S("kv_up"), 1)

            conv_in(0)
            pe.wait_ge(S("ckv_done"), 3)
            pe.wait_ge(S("ql_done"), 3)
            for c, (r, n) in enumerate(CHUNKS):
                for l in range(2):
                    tr(PS[2 + c // 2][:, 256 * (c % 2) + 128 * l:256 * (c % 2) + 128 * l + n],
                       ckv[0:n, c, LAT + 128 * l:LAT + 128 * l + 128], n)
            tr(PS[3][:, 256:256 + NS], ckv[0:NS, 2, 0:128], NS)
            for c in ORDER:
                n = CHUNKS[c][1]
                for j in range(3):
                    dst = PS[3][:, 320 + NS * j:320 + NS * j + NS] if c == 2 else PS[4 + c][:, 128 * j:128 * j + n]
                    last = tr(dst, ql[0:n, c, 128 * j:128 * j + 128], n)
                last.then_inc(S("ql_T"), 1)
            conv_in(1)
            q_up(0)
            pe.wait_ge(S("wkv_in"), 64)
            pe.wait_ge(S("latT"), 3)
            for hp in range(4):
                for l in range(2):
                    last = tr(PS[2 + hp // 2][:, 256 * (hp % 2) + 128 * l:256 * (hp % 2) + 128 * l + 128],
                              wk[:, l, 128 * hp:128 * hp + 128])
            last.then_inc(S("wk_T"), 1)
            conv_in(2)
            pe.wait_ge(S("wkT"), 2)
            kv_up(0)
            q_up(1)
            conv_in(3)
            pe.wait_ge(S("q_done"), 1)
            pe.wait_ge(S("k_sq"), 1)
            for hp in range(4):
                tr(PS[3][:, 64 * hp:64 * hp + 64], qsn[0:NS, 128 * hp:128 * hp + 128], NS)
            for h in range(H):
                last = tr(PS[2][:, 64 * h:64 * h + 64], qsr[0:NS, 32 * h:32 * h + 128], NS)
            last.then_inc(S("qs_T"), 1)
            kv_up(1)
            pe.wait_ge(S("qsT"), 1)
            for l in range(2):
                for hp in range(4):
                    last = mm(PS[2 + l][:, 128 * hp:128 * hp + 128], wkT[:, hp, 128 * l:128 * l + 128], qsT[:, hp, :], True, True)
            last.then_inc(S("q_abs"), 1)
            q_up(2)
            pe.wait_ge(S("qabs"), 2)
            for l in range(2):
                mm(PS[2][0:NS, :], ckvT[:, l, SEQ:T], qabs[:, l, :], l == 0, False)
            mm(PS[2][0:NS, :], krn[:], qrT[:], False, True).then_inc(S("s_new"), 1)
            kv_up(2)
            for i in range(4):
                c, src = ((0, kt), (0, qt), (1, kt), (1, qt))[i]
                pe.wait_ge(S("k_done"), 2 + c)
                pe.wait_ge(S("q_done"), 2 + c)
                if i == 0:
                    pe.wait_ge(S("snew"), 1)
                    pe.wait_ge(S("v_done"), 1)
                for hb in range(2):
                    b = 2 * i + hb
                    if i >= 2:
                        pe.wait_ge(S("heads_ev"), b - 3)
                    for h in range(4):
                        last = tr(PS[(2, 3, 6, 7)[b % 4]][0:DQ, 128 * h:128 * h + 128],
                                  src[c][:, DQ * (4 * hb + h):DQ * (4 * hb + h) + DQ])
                    last.then_inc(S("heads_T"), 1)
            pe.wait_ge(S("v_done"), 2)
            for c in range(CC):
                tr(PS[1][0:W - 1, 128 * c:128 * c + 128], glu[:, c, SEQ:SEQ + W - 1])
            for c in range(CC):
                last = tr(PS[0][0:NS, 128 * c:128 * c + 128], gpk[:, c, :])
            last.then_inc(S("rows_T"), 1)

            pe.wait_ge(S("heads_ev"), 8)
            pe.wait_ge(S("rows_ev"), 1)
            pe.wait_ge(S("snew"), 1)

            def part_max(n):
                pe.wait_ge(S("m_part"), n + 1)
                tr(PS[6][:, 0:128], m1[:]).then_inc(S("m_T"), 1)

            def part_spread(n):
                pe.wait_ge(S("m_diag"), n + 1)
                mm(PS[6][:, 128:256], ones, dg[:], True, True).then_inc(S("m_all"), 1)

            def part_out(n, t):
                pe.wait_ge(S("probs"), n + 1)
                for b in range(PAGES):
                    mm(PS[7][0:64, 0:260], s_all[t][:, b, :], ck[t][:, b, ONE:CROW], b == 0, False)
                mm(PS[7][0:64, 0:260], pn[:], ckv[:, 2, ONE:CROW], False, True).then_inc(S("ck_used"), 1)

            def part_outT(n):
                pe.wait_ge(S("oc_n"), n + 1)
                for l in range(2):
                    last = tr(PS[6][:, 256 + 128 * l:384 + 128 * l], ocn[:, 128 * l:128 * l + 128])
                last.then_inc(S("oc_T"), 1)

            def sequence(n, t, first):
                pair = n - t
                def transposes(b):
                    m = n * PAGES + b
                    if b == PAGES // 2:
                        pe.wait_ge(S(f"ck2_in{t}"), page_count(n, t))
                    if not (first and b < 2):
                        pe.wait_ge(S("cT"), m - 1)
                    tr(PS[b % 2][:, 0:128], ck[t][:, b, LAT:LAT + 128])
                    tr(PS[b % 2][:, 128:256], ck[t][:, b, LAT + 128:CROW])
                    tr(PS[b % 2][:, 256:384], ck[t][:, b, 0:128]).then_inc(S("c_T"), 1)
                pe.wait_ge(S(f"ck_in{t}"), page_count(n, t))
                if first:
                    pe.wait_ge(S("ck_ones"), 1)
                transposes(0)
                for b in range(PAGES):
                    m = n * PAGES + b
                    if b < PAGES - 1:
                        transposes(b + 1)
                    pe.wait_ge(S("cT"), m + 1)
                    if not (first and b < 2):
                        pe.wait_ge(S("sq"), m - 1)
                    for l in range(2):
                        last = mm(PS[2 + b % 2][:, :], cT[:, b % 2, 128 * l:128 * l + 128], wk[:, l, :], l == 0, l == 1)
                    last.then_inc(S("keys"), 1)
                    half = PS[4 + b // 4][:, 128 * (b % 4):128 * (b % 4) + 128]
                    if b % 4 == 0 and not first:
                        pe.wait_ge(S("s_half"), 2 * n + b // 4 - 1)
                    cols = bass.ds(pair * 64, 128)
                    for l in range(2):
                        mm(half, cT[:, b % 2, 128 * l:128 * l + 128], qabs[:, l, cols], l == 0, False)
                    mm(half, cT[:, b % 2, 256:384], qrT[:, cols], False, True).then_inc(S("scores"), 1)
                    if not first:
                        if b == 1:
                            part_max(n - 1)
                        if b == 2:
                            part_spread(n - 1)
                        if b == 4:
                            part_out(n - 1, 1 - t)
                        if b == 6:
                            part_outT(n - 1)
            sequence(0, 0, True)
            with pe.Fori(0, 3) as i:
                sequence(2 * i + 1, 1, False)
                sequence(2 * i + 2, 0, False)
            sequence(7, 1, False)
            part_max(7)
            part_spread(7)
            part_out(7, 1)
            part_outT(7)

            def p_scores(h):
                if h >= 2:
                    pe.wait_ge(S("p_s"), h - 1)
                mm(PS[h % 2][:, 0:128], qT[0:DQ, h, 0:128], kT[0:DQ, h, 0:128], True, True)
                mm(PS[h % 2][:, 128:384], qT[0:DQ, h, 128:256], kT[0:DQ, h, :], True, True).then_inc(S("p_sc"), 1)

            def p_trans(h):
                pe.wait_ge(S("p_exp"), h + 1)
                if h >= 2:
                    pe.wait_ge(S("p_T"), h - 1)
                for j in range(3):
                    last = tr(PS[2 + h % 2][:, 128 * j:128 * j + 128], pr[h % 2][:, j, :])
                last.then_inc(S("p_tr"), 1)

            def p_out(h):
                pe.wait_ge(S("p_T"), h + 1)
                if h >= 2:
                    pe.wait_ge(S("p_o"), h - 1)
                v = slice(DV * h, DV * h + 128)
                mm(PS[4 + h % 2][:, 0:128], pT[h % 2][:, 0, :], vt[:, 0, v], True, True)
                mm(PS[4 + h % 2][:, 128:256], pT[h % 2][:, 1, :], vt[:, 0, v], True, False)
                mm(PS[4 + h % 2][:, 128:256], pT[h % 2][:, 2, :], vt[:, 1, v], False, True).then_inc(S("p_out"), 1)
            pe.wait_ge(S("s_half"), 2 * DEC_B)
            pe.wait_ge(S("sq"), PAGES * DEC_B)
            for h in range(H + 2):
                if h < H:
                    p_scores(h)
                if 1 <= h <= H:
                    p_trans(h - 1)
                if h >= 2:
                    p_out(h - 2)
                if h == 1:
                    pe.wait_ge(S("ocT"), DEC_B)
                    for hh in range(H):
                        for l in range(2):
                            last = mm(PS[7][0:NS, DV * hh:DV * hh + DV], ocT[:, l, 64 * hh:64 * hh + 64],
                                      wv[:, l, DV * hh:DV * hh + DV], l == 0, l == 1)
                    last.then_inc(S("attn_s"), 1)
            def mix_T(src, ready, c, bank):
                n = CHUNKS[c][1]
                pe.wait_ge(S(ready), c + 1)
                for j in range(CC):
                    last = tr(bank[:, 128 * j:128 * j + n], src[0:n, c, 128 * j:128 * j + 128], n)
                last.then_inc(S("mix_T"), 1)

            pe.wait_ge(S("conv_done"), 1)
            pe.wait_ge(S("p_T"), H)
            pe.wait_ge(S("attn_done"), 1)
            for c in range(NC):
                for j in range(CC):
                    last = tr(PS[(6, 7, 3)[c]][:, 128 * j:128 * j + 128], acc[:, j, 128 * c:128 * c + 128])
                last.then_inc(S("conv_T"), 1)
            pe.wait_ge(S("p_s"), H)
            for c in range(NC):
                mix_T(attn_t, "attn_n", c, PS[c])
            pe.wait_ge(S("wout_in"), 16)
            pe.wait_ge(S("p_o"), H)
            pe.wait_ge(S("mixT"), 3)

            def merge(c, hf, ks):
                r, n = CHUNKS[c]
                for k in ks:
                    last = mm(PS[(4, 0, 2)[c] + hf][0:n, :], xT[:, k, r:r + n], wout[:, k, 512 * hf:512 * hf + 512],
                              k == 4, k == 3)
                return last
            for c in range(NC):
                for hf in range(2):
                    if c == 2 and hf == 1:
                        pe.wait_ge(S("ln"), 3)
                    merge(c, hf, range(4, 8))
            for c in range(NC):
                if c == 2:
                    pe.wait_ge(S("mixT"), 4)
                mix_T(conv_t, "conv_n", c, PS[(6, 7, 6)[c]])
            for c in range(NC):
                pe.wait_ge(S("mixT"), 4 + c)
                for hf in range(2):
                    merge(c, hf, range(4)).then_inc(S("merged"), 1)
            for g in range(6):
                c, n = g // 2, CHUNKS[g // 2][1]
                pe.wait_ge(S("xn2"), c + 1)
                if g == 0:
                    pe.wait_ge(S("mixT"), 6)
                b = (0, 1, 4, 5, 6, 7)[g]
                for j in range(4):
                    k = 4 * (g % 2) + j
                    last = tr(PS[b][:, 128 * j:128 * j + n], xn2[0:n, c, 128 * k:128 * k + 128], n)
                last.then_inc(S("h_T"), 1)
            pe.wait_ge(S("hT"), 6)
            pe.wait_ge(S("wr_in"), 32)
            for k in range(KD):
                last = mm(PS[2][0:NE, 0:T], wr[:, k, :], xT[:, k, :], k == 0, k == KD - 1)
            last.then_inc(S("route_mm"), 1)
            pe.wait_ge(S("lgT"), 1)
            for c in range(NC):
                last = tr(PS[3][:, 32 * c:32 * c + 32], lgT[:, 128 * c:128 * c + 128], 32)
            last.then_inc(S("route_mm"), 1)
            pe.wait_ge(S("routed"), 1)
            for c in range(NC):
                for cc in range(c + 1):
                    last = mm(PS[0][:, 32 * c:32 * c + 32], upper if cc == c else ones, M[:, cc, :], cc == 0, cc == c)
            for c in range(NC):
                last = mm(PS[1][0:NE, 0:128], M[:, c, :], ones, c == 0, c == NC - 1)
            last.then_inc(S("route_mm"), 1)
            pe.wait_ge(S("routed"), 2)
            mm(PS[2][0:NE, 0:128], upper[0:NE, 0:NE], extra[:], True, True)
            mm(PS[4][0:1, 0:128], ones[0:NE, 0:1], extra[:], True, True).then_inc(S("route_mm"), 1)
            for c in range(NC):
                tr(PS[5][0:NE, 128 * c:128 * c + 128], posI[:, c, 0:NE])
                last = tr(PS[6][0:NE, 128 * c:128 * c + 128], G[:, c, :])
            last.then_inc(S("route_mm"), 1)
            pe.wait_ge(S("routed"), 3)
            pe.wait_ge(S("routed"), 4)
            for c in range(NC):
                cs = slice(128 * c, 128 * c + 128)
                mm(PS[7][:, 64 * c:64 * c + 64], posT[:, cs], P[:], True, False)
                mm(PS[7][:, 64 * c:64 * c + 64], ones[0:NE, :], tmpP[:], False, True)
                mm(PS[3][:, 64 * c:64 * c + 64], GT[0:NE, cs], P[:], True, True)
            mm(PS[4][0:1, 128:192], pidx[0:NE, :], P[:], True, True).then_inc(S("route_mm"), 1)
            pe.wait_ge(S("bdn_in"), 16)
            for c in range(NC):
                for hf in range(2):
                    if 2 * c + hf >= 2:
                        pe.wait_ge(S("ybias"), 2 * c + hf - 1)
                    mm(PS[hf][:, :], GT[:, 128 * c:128 * c + 128], bdn[:, 512 * hf:512 * hf + 512], True, True)\
                        .then_inc(S("y_bias"), 1)

            def gather(v):
                pe.wait_ge(S("sel"), v)
                for k in range(KD):
                    for c in range(NC):
                        last = mm(PS[5 + k // 4][:, 128 * (k % 4):128 * (k % 4) + 128],
                                  xn2[:, c, 128 * k:128 * k + 128], sel[:, c, :], c == 0, c == NC - 1)
                last.then_inc(S("gathered"), 1)

            def gate_up(i, t):
                n = 2 * i + t
                if t == 0:
                    pe.wait_ge(S("xg"), i + 1)
                pe.wait_ge(S(f"bias_in{t}"), 16 * i + 16)
                pe.wait_ge(S("gu_ev"), n + 1)
                xs = [xg[:, k, 64 * t:64 * t + 64] for k in range(KD)]
                for q in range(4):
                    last = mm(PS[q // 2][64 * (q % 2):64 * (q % 2) + 64, :], one_row,
                              bias[t][:, 512 * q:512 * q + 512], True, False)
                last.then_inc(S(f"bias_used{t}"), 1)
                for k in range(KD):
                    if k % 2 == 0:
                        pe.wait_ge(S(f"gu_in{k // 2}"), 32 * i + 16 * t + 16)
                    for q in range(4):
                        last = mm(PS[q // 2][64 * (q % 2):64 * (q % 2) + 64, :], xs[k],
                                  gu_ring[:, k, 512 * q:512 * q + 512], False, k == KD - 1)
                    if k == KD - 1:
                        last.then_inc(S("gu_done"), 1)
                    if k % 2 == 1 and k < KD - 1:
                        last.then_inc(S(f"gu_used{k // 2}"), 1)

            def combine(v):
                pe.wait_ge(S("selT"), v + 1)
                pe.wait_ge(S("y_ev"), 2 * v + 2)
                for c in range(NC):
                    for hf in range(2):
                        q = 2 * c + hf
                        if q >= 3:
                            pe.wait_ge(S("y_add"), 6 * v + q - 2)
                        mm(PS[5 + q % 3][:, :], selT[:, hf, 128 * c:128 * c + 128], ysb[:, hf, :], True, True)\
                            .then_inc(S("combined"), 1)

            def down(i, t):
                n = 2 * i + t
                pe.wait_ge(S("h"), n + 1)
                for c in range(4):
                    last = tr(PS[4][:, 128 * c:128 * c + 128], hsb[:, 128 * c:128 * c + 128])
                last.then_inc(S("h_tr"), 1)
                pe.wait_ge(S("h_ev"), n + 1)
                for k in range(KD):
                    if k % 4 == 0:
                        pe.wait_ge(S(f"dn_in{k // 4}"), 32 * i + 16 * t + 16)
                    lhsT = hT[:, 128 * (k % 4) + 64 * (k // 4):128 * (k % 4) + 64 * (k // 4) + 64]
                    for hf in range(2):
                        p = 64 * (t ^ hf)
                        last = mm(PS[2 + hf][p:p + 64, :], lhsT, dn_ring[:, k, 512 * hf:512 * hf + 512], k == 0, k == KD - 1)
                    if k == 3:
                        last.then_inc(S("dn_used0"), 1)
                last.then_inc(S("dn_done"), 1)

            gsb_, usb_, sgb_, hsb, hT = gsb
            pe.wait_ge(S("ybias"), 6)
            pe.wait_ge(S("tab_ev"), 1)
            pe.wait_ge(S("moe_zero"), 1)
            gather(1)
            pe.wait_ge(S("table"), 1)
            n_iter = pe.value_load(tab[0:1, 0:1], min_val=NE // 2, max_val=MAX_ITER)
            with pe.Fori(0, n_iter) as i:
                gate_up(i, 0)
                combine(i)
                down(i, 0)
                gate_up(i, 1)
                pe.wait_ge(S("selg"), i + 1)
                pe.wait_ge(S("h_ev"), 2 * i + 1)
                pe.wait_ge(S("y_add"), 6 * i + 6)
                for c in range(NC):
                    tr(PS[4][:, 128 * c:128 * c + 128], selg[:, c, 0:128])
                    last = tr(PS[7][:, 128 * c:128 * c + 128], selg[:, c, 64:192])
                last.then_inc(S("sel_T"), 1)
                gather(i + 2)
                pe.wait_ge(S("selT"), i + 2)
                down(i, 1)
            pe.wait_ge(S("xg"), n_iter + 1)
            combine(n_iter)

        @block.scalar
        def _(act):
            act.dma_start(cst[:], c_pack).then_inc(S("cst_in"), 16)
            act.dma_start(rows2[0:8, :], norm_mix[0].rearrange("(k p) -> k p", p=128)).then_inc(S("rows_in"), 16)
            act.dma_start(rows2[8:11, :], norm_q_lat[0].rearrange("(k p) -> k p", p=128)).then_inc(S("rows_in"), 16)
            act.dma_start(rows2[11:15, :], conv_b[0].rearrange("(k p) -> k p", p=128)).then_inc(S("rows_in"), 16)
            act.dma_start(rows2[15:19, :], norm_out_conv[0].rearrange("(k p) -> k p", p=128)).then_inc(S("rows_in"), 16)
            act.dma_start(rows2[19:23, :], norm_out_attn[0].rearrange("(k p) -> k p", p=128)).then_inc(S("rows_in"), 16)
            act.dma_start(rows2[23:31, :], norm_ffn[0].rearrange("(k p) -> k p", p=128)).then_inc(S("rows_in"), 16)
            act.dma_start(rows1[:], conv_w[0].rearrange("t (c p) -> (t c) p", p=128)).then_inc(S("rows_in"), 16)
            act.dma_start(cos[:], c_cos).then_inc(S("rope_in"), 16)
            act.dma_start(sin[:], c_sin).then_inc(S("rope_in"), 16)
            act.dma_start(gkv[:], norm_kv_lat[0:1].partition_broadcast(128)).then_inc(S("g_in"), 16)
            for g, src in ((gqk, norm_qk_q), (gkk, norm_qk_k)):
                act.dma_start(g[:, 0:80], src[0:1].partition_broadcast(128)).then_inc(S("g_in"), 16)
                act.dma_start(g[:, 80:96], src[0:1, 64:80].partition_broadcast(128)).then_inc(S("g_in"), 16)
            for i in range(2):
                act.dma_start(st_rows[:, i, :], state_conv[0, 4 * i:4 * i + 4].rearrange("b t c -> (b t) c")).then_inc(S("st_in"), 16)
            act.preload_act_table_set("natural_log_exp_and_others")

            def copy(out, in_):
                return act.activation(out, in_, ACT.Copy)

            def root(out, in_, scale, own_input=True):
                p, tmp = in_.shape[0], lnx
                k = 1
                for d in in_.shape[1:]:
                    k *= d
                tmp = lnx[0:p, 0:k]
                if len(in_.shape) == 3:
                    tmp = tmp.rearrange("p (a b) -> p a b", a=in_.shape[1])
                if own_input:
                    act.drain()
                act.activation(tmp, in_, ACT.Ln, bias=eps[0:p, :], scale=scale)
                act.drain()
                return act.activation(out, tmp, ACT.Exp, scale=-0.5)

            sq_x = view(R_GU + NC * QL + 2 * T + 3 * T + 2 * T, D)
            act.wait_ge(S("cst_in"), 16)
            act.wait_ge(S("x_in"), 32)
            act.wait_ge(S("zeroed"), 1)
            for c, (r, n) in enumerate(CHUNKS):
                act.drain()
                act.activation(sq_x[0:n], X[0:n, c, :], ACT.Square, accum_out=ss[0:n, c:c + 1])
            root(rs[:, 0:3], ss[:, 0:3], 1 / D).then_inc(S("root"), 1)
            for i, c in enumerate(ORDER):
                n = CHUNKS[c][1]
                act.wait_ge(S("proj_done"), i + 1)
                act.activation(sq_x[0:n, 0:QL], PS[2 * c][0:n, 0:QL], ACT.Square, accum_out=ss[0:n, 4 + 2 * c:5 + 2 * c])
                act.activation(sq_x[0:n, 512:768], PS[2 * c + 1][0:n, 0:KVL], ACT.Square, accum_out=ss[0:n, 5 + 2 * c:6 + 2 * c])
                act.drain()
                act.activation(lnx[0:n, 0:1], ss[0:n, 4 + 2 * c:5 + 2 * c], ACT.Ln, bias=eps[0:n, :], scale=1 / QL)
                act.activation(lnx[0:n, 1:2], ss[0:n, 5 + 2 * c:6 + 2 * c], ACT.Ln, bias=eps[0:n, :], scale=1 / KVL)
                act.drain()
                act.activation(rs[0:n, 4 + 2 * c:6 + 2 * c], lnx[0:n, 0:2], ACT.Exp, scale=-0.5).then_inc(S("rl"), 1)

            def gate_exp(c):
                act.wait_ge(S("proj_done"), 3 + 2 * c + 1)
                if c >= 2:
                    act.wait_ge(S("glu"), c - 1)
                act.activation(eg[:, c % 2, :], PS[7 if c % 2 == 0 else 1][:, 0:T], ACT.Exp, scale=-1.0).then_inc(S("eg"), 1)

            def q_copy(i):
                c = ORDER[i]
                n = CHUNKS[c][1]
                act.wait_ge(S("q_up"), i + 1)
                q = qt[c][0:n].rearrange("p (h d) -> p h d", h=H)
                for hb in range(2):
                    src = PS[4 + hb][0:n, 0:384].rearrange("p (h d) -> p h d", h=4)
                    copy(q[:, 4 * hb:4 * hb + 4, 0:DN], src[:, :, 0:DN]).then_inc(S("q_nope"), 1)

            def q_root(i):
                c = ORDER[i]
                n = CHUNKS[c][1]
                act.wait_ge(S("q_rope"), i + 1)
                act.activation(sqs[0:n, 0, :], qt[c][0:n], ACT.Square).then_inc(S("q_sq"), 1)
                act.wait_ge(S("q_ss"), i + 1)
                root(r8[0:n, 0, :], s8[0:n, 0, :], 1 / DQ).then_inc(S("q_r"), 1)

            def k_root(i):
                c = ORDER[i]
                n = CHUNKS[c][1]
                act.wait_ge(S("kv_up"), i + 1)
                act.activation(sqs[0:n, 1, 0:512], PS[(2, 6, 0)[i]][0:n, :], ACT.Square).then_inc(S("k_sq"), 1)
                if i:
                    copy(vt[:, c, 0:512], PS[(7, 1)[i - 1]][:, :]).then_inc(S("v_done"), 1)
                act.wait_ge(S("k_ss"), i + 1)
                root(r8[0:n, 1 if i else 2, :], s8[0:n, 1, :], 1 / DQ).then_inc(S("k_r"), 1)

            gate_exp(0)
            gate_exp(1)
            q_copy(0)
            act.wait_ge(S("wk_T"), 1)
            for j in range(2):
                copy(wkT[:, 2 * j:2 * j + 2, :], PS[2 + j][:, :].rearrange("p (a b) -> p a b", a=2)).then_inc(S("wkT"), 1)
            q_root(0)
            gate_exp(2)
            k_root(0)
            q_copy(1)
            q_root(1)
            gate_exp(3)
            k_root(1)
            q_copy(2)
            q_root(2)
            k_root(2)
            act.wait_ge(S("rows_T"), 1)
            copy(row_out[:], PS[0][0:NS, :])
            copy(row_out2[0:W - 1, :], PS[1][0:W - 1, :])
            act.drain()
            act.nop().then_inc(S("rows_ev"), 1)

            def rk(n, half):
                act.wait_ge(S("ss_half"), 2 * n + half + 1)
                root(r8[:, 4 * half:4 * half + 4, :], s8[:, 4 * half:4 * half + 4, :], 1 / DQ, False).then_inc(S("rk"), 1)

            def probs(n, t):
                act.wait_ge(S("s_sub"), n + 1)
                act.activation(s_all[t], s_all[t], ACT.Exp, scale=SCALE)
                act.activation(pn[0:NS, :], pn[0:NS, :], ACT.Exp, scale=SCALE).then_inc(S("probs"), 1)

            def sequence(n, t, first):
                def take_T(b):
                    m = n * PAGES + b
                    act.wait_ge(S("c_T"), m + 1)
                    if not (first and b < 2):
                        act.wait_ge(S("scores"), m - 1)
                    copy(cT[:, b % 2, :], PS[b % 2][:, 0:384]).then_inc(S("cT"), 1)
                take_T(0)
                for b in range(PAGES):
                    m = n * PAGES + b
                    if b < PAGES - 1:
                        take_T(b + 1)
                    act.wait_ge(S("keys"), m + 1)
                    if not (first and b < 2):
                        act.wait_ge(S("kss"), m - 1)
                    act.activation(sqk[b % 2], PS[2 + b % 2][:, :], ACT.Square).then_inc(S("sq"), 1)
                    if b == 0 and not first:
                        rk(n - 1, 1)
                    if b == 3 and not first:
                        probs(n - 1, 1 - t)
                    if b == 4:
                        rk(n, 0)
            sequence(0, 0, True)
            with act.Fori(0, 3) as i:
                sequence(2 * i + 1, 1, False)
                sequence(2 * i + 2, 0, False)
            sequence(7, 1, False)
            rk(7, 1)
            probs(7, 1)

            def p_exp(h):
                act.wait_ge(S("p_m"), h + 1)
                if h >= 2:
                    act.wait_ge(S("p_o"), h - 1)
                act.activation(pr[h % 2][:, 0, :], pr[h % 2][:, 0, :], ACT.Exp, bias=pm[:, h % 2, 0:1], scale=SCALE,
                               accum_out=psm[:, h % 2, 0:1])
                act.activation(pr[h % 2][:, 1:3, :], pr[h % 2][:, 1:3, :], ACT.Exp, bias=pm[:, h % 2, 1:2], scale=SCALE,
                               accum_out=psm[:, h % 2, 1:2])
                act.drain()
                act.nop().then_inc(S("p_exp"), 1)

            def p_T(h):
                act.wait_ge(S("p_tr"), h + 1)
                if h >= 2:
                    act.wait_ge(S("p_out"), h - 1)
                copy(pT[h % 2], PS[2 + h % 2][:, 0:384].rearrange("p (a b) -> p a b", a=3)).then_inc(S("p_T"), 1)
            for h in range(H + 1):
                if h < H:
                    p_exp(h)
                if h >= 1:
                    p_T(h - 1)
            scr = view(R_C, NC * DC)
            ez = view(R_C, NC, DC)
            act.wait_ge(S("p_o"), H)
            act.wait_ge(S("attn_done"), 1)
            act.wait_ge(S("conv_done"), 1)
            for c, (r, n) in enumerate(CHUNKS):
                act.activation(scr[0:n, DC * c:DC * c + DC], attn_t[0:n, c, :], ACT.Square, accum_out=ss[0:n, c:c + 1])
            root(rs[:, 0:3], ss[:, 0:3], 1 / DC).then_inc(S("root"), 1)
            act.wait_ge(S("mv"), 1)
            root(rs[:, 3:6], mv[:, :, 1], 1.0).then_inc(S("root"), 1)
            act.wait_ge(S("ln"), 4)
            act.activation(ez, conv_t, ACT.Exp, scale=-1.0).then_inc(S("ez"), 1)
            act.wait_ge(S("ln"), 5)
            for c in range(NC):
                act.activation(scr[:, DC * c:DC * c + DC], conv_t[:, c, :], ACT.Square, accum_out=ss[:, 6 + c:7 + c])
            root(rs[:, 6:9], ss[:, 6:9], 1 / DC).then_inc(S("root"), 1)
            act.wait_ge(S("h_rows"), NC)
            act.wait_ge(S("conv_n"), 3)
            for c, (r, n) in enumerate(CHUNKS):
                act.drain()
                act.activation(scr[0:n, 0:D], X[0:n, c, :], ACT.Square, accum_out=ss[0:n, 9 + c:10 + c])
            root(rs[:, 9:12], ss[:, 9:12], 1 / D).then_inc(S("root"), 1)
            act.wait_ge(S("gate_d"), 1)
            act.activation(gate4[:], gate4[:], ACT.Exp).then_inc(S("gate_e"), 1)

            gsb_, usb_, sgb_, hsb, hT = gsb
            act.preload_act_table(ACT.Sigmoid)

            def sigmoid(i, t):
                act.wait_ge(S("g_min"), 2 * i + t + 1)
                act.activation(sgb_, gsb_, ACT.Sigmoid, scale=ALPHA).then_inc(S("sig"), 1)

            def h_rows_T(i, t):
                act.wait_ge(S("h_tr"), 2 * i + t + 1)
                copy(hT, PS[4][:, :]).then_inc(S("h_ev"), 1)

            def y_rows(i, t):
                act.wait_ge(S("dn_done"), 2 * i + t + 1)
                if t == 0:
                    act.wait_ge(S("combined"), 6 * i + 6)
                copy(ysb[64 * t:64 * t + 64, 0, :], PS[2][64 * t:64 * t + 64, :])
                u = 64 * (1 - t)
                copy(ysb[u:u + 64, 1, :], PS[3][u:u + 64, :]).then_inc(S("y_ev"), 1)

            act.wait_ge(S("table"), 1)
            n_iter = act.value_load(tab[0:1, 0:1], min_val=NE // 2, max_val=MAX_ITER)
            with act.Fori(0, n_iter) as i:
                sigmoid(i, 0)
                h_rows_T(i, 0)
                y_rows(i, 0)
                sigmoid(i, 1)
                act.wait_ge(S("sel_T"), i + 1)
                copy(selT[:, 0, :], PS[4][:, 0:384])
                copy(selT[:, 1, :], PS[7][:, 0:384]).then_inc(S("selT"), 1)
                h_rows_T(i, 1)
                y_rows(i, 1)

        @block.vector
        def _(dve):
            def tt(out, a, b, op):
                return dve.tensor_tensor(out, a, b, op)

            def ts(out, a, s1, s2=None, op0=ALU.mult, op1=ALU.mult):
                return dve.tensor_scalar(out, a, s1, s2, op0, op1) if s2 is not None else dve.tensor_scalar(out, a, s1, None, op0)

            dve.wait_ge(S("gains_T"), 1)
            dve.wait_ge(S("zeroed"), 1)
            dve.tensor_copy(cw[:, 0:124], PS[7][:, 0:124])
            dve.tensor_copy(gc[:], PS[7][:, 128:159]).then_inc(S("gains"), 1)
            dve.wait_ge(S("g_in"), 80)
            tt(gqk[:], gqk[:], gkk[:], ALU.mult)
            dve.wait_ge(S("root"), 1)
            for c, (r, n) in enumerate(CHUNKS):
                ts(xn[0:n, c, :], X[0:n, c, :], rs[0:n, c:c + 1]).then_inc(S("xn"), 1)
            dve.wait_ge(S("gains"), 1)
            for g in range(6):
                c, (r, n) = g // 2, CHUNKS[g // 2]
                k = 4 * (g % 2)
                dve.wait_ge(S("x_T"), g + 1)
                tt(xT[:, k:k + 4, r:r + n], PS[g][:, :].rearrange("p (a b) -> p a b", a=4)[:, :, 0:n],
                   bc(g_mix[:, k:k + 4], [128, 4, n], 2), ALU.mult).then_inc(S("xT"), 1)
            dve.wait_ge(S("state_T"), 1)
            dve.wait_ge(S("conv_zero"), 1)

            def seg(c, a, b):
                return glu[:, c, SEG0:GLU_W].rearrange("p (s u) -> p s u", u=SEG)[:, :, a:b]
            for c in range(CC):
                dve.tensor_copy(seg(c, 0, W - 1), PS[6 + c // 2][:, 256 * (c % 2):256 * (c % 2) + 240]
                                .rearrange("p (s u) -> p s u", u=W - 1)).then_inc(S("state_ev"), 1)
            for c in range(CC):
                ts(acc[:, c, 0:SEQ], acc[:, c, 0:SEQ], g_cb[:, c:c + 1], None, ALU.add)

            def rotate(out1, out2, v, cs, sn, shape, tmp):
                k = 1
                for d in shape[1:]:
                    k *= d
                n = shape[0]
                ta, tb = rope_a[0:n, tmp:tmp + k], rope_b[0:n, tmp:tmp + k]
                if len(shape) == 4:
                    ta, tb = (z.rearrange("p (a b c) -> p a b c", a=shape[1], b=2) for z in (ta, tb))
                else:
                    ta, tb = (z.rearrange("p (b c) -> p b c", b=2) for z in (ta, tb))
                tt(ta, v, cs, ALU.mult)
                tt(tb, v, sn, ALU.mult)
                dve.drain()
                if len(shape) == 4:
                    a1, a2, b1, b2 = ta[:, :, 0, :], ta[:, :, 1, :], tb[:, :, 0, :], tb[:, :, 1, :]
                else:
                    a1, a2, b1, b2 = ta[:, 0, :], ta[:, 1, :], tb[:, 0, :], tb[:, 1, :]
                tt(out1, a1, b2, ALU.subtract)
                return tt(out2, a2, b1, ALU.add)

            dve.wait_ge(S("rope_in"), 32)
            dve.wait_ge(S("zeroed"), 3)
            for i, c in enumerate(ORDER):
                n = CHUNKS[c][1]
                dve.wait_ge(S("rl"), i + 1)
                ts(ql[0:n, c, :], PS[2 * c][0:n, 0:QL], rs[0:n, 4 + 2 * c:5 + 2 * c]).then_inc(S("ql_done"), 1)
                kv = PS[2 * c + 1]
                dve.scalar_tensor_tensor(ckv[0:n, c, LAT:CROW], kv[0:n, 0:KVL], rs[0:n, 5 + 2 * c:6 + 2 * c], gkv[0:n, :],
                                         ALU.mult, ALU.mult)
                dve.drain()
                rotate(ckv[0:n, c, 0:16], ckv[0:n, c, 16:32], kv[0:n, KVL:288].rearrange("p (b c) -> p b c", b=2),
                       bc(cos[0:n, c, :], [n, 2, 16], 1), bc(sin[0:n, c, :], [n, 2, 16], 1), [n, 2, 16], 0)
                dve.drain()
                dve.engine_nop().then_inc(S("ckv_done"), 1)

            def gated(c):
                e, a = eg[:, c % 2, :], PS[6 if c % 2 == 0 else 0]
                dve.wait_ge(S("eg"), c + 1)
                ts(e, e, 1.0, None, ALU.add)
                dve.drain()
                dve.reciprocal(e, e)
                dve.drain()
                dve.wait_ge(S("proj_done"), 3 + 2 * c + 2)
                tt(glu[:, c, W - 1:SEG0], a[:, 0:SEQ], e[:, 0:SEQ], ALU.mult)
                tt(gpk[:, c, :], a[:, SEQ:T], e[:, SEQ:T], ALU.mult)
                dve.drain()
                dve.tensor_copy(seg(c, W - 1, SEG - 1), gpk[:, c, :].rearrange("p (s q) -> p s q", s=DEC_B)).then_inc(S("glu"), 1)

            def q_rotate(i):
                c = ORDER[i]
                n = CHUNKS[c][1]
                q = qt[c][0:n].rearrange("p (h d) -> p h d", h=H)
                for hb in range(2):
                    dve.wait_ge(S("q_nope"), 2 * i + hb + 1)
                    v = PS[4 + hb][0:n, 0:384].rearrange("p (h d) -> p h d", h=4)[:, :, DN:DQ]
                    v = v.rearrange("p h (b c) -> p h b c", b=2)
                    hs = slice(4 * hb, 4 * hb + 4)
                    cs, sn = (z[0:n, c, :].unsqueeze(1).unsqueeze(1).broadcast_to([n, 4, 2, 16]) for z in (cos, sin))
                    dve.drain()
                    rotate(q[:, hs, DN:DN + 16], q[:, hs, DN + 16:DQ], v, cs, sn, [n, 4, 2, 16], 0)
                dve.drain()
                dve.engine_nop().then_inc(S("q_rope"), 1)

            def q_norm(i):
                c = ORDER[i]
                n = CHUNKS[c][1]
                q = qt[c][0:n].rearrange("p (h d) -> p h d", h=H)
                dve.wait_ge(S("q_sq"), i + 1)
                dve.tensor_reduce(s8[0:n, 0, :], sqs[0:n, 0, :].rearrange("p (h d) -> p h d", h=H), X_AXIS, ALU.add)\
                    .then_inc(S("q_ss"), 1)
                dve.wait_ge(S("q_r"), i + 1)
                tt(q, q, bc(r8[0:n, 0, :], [n, H, DQ], 2), ALU.mult)
                dve.drain()
                if i:
                    tt(q, q, bc(gqk[0:n, :], [n, H, DQ], 1), ALU.mult).then_inc(S("q_done"), 1)
                else:
                    tt(qsn[0:n].rearrange("p (h d) -> p h d", h=H), q[:, :, 0:DN], bc(gqk[0:n, 0:DN], [n, H, DN], 1), ALU.mult)
                    tt(qsr[0:n, 0:256].rearrange("p (h d) -> p h d", h=H), q[:, :, DN:DQ],
                       bc(gqk[0:n, DN:DQ], [n, H, DR], 1), ALU.mult)
                    dve.drain()
                    dve.engine_nop().then_inc(S("q_done"), 1)

            def k_sums(i):
                c = ORDER[i]
                n = CHUNKS[c][1]
                kr = ckv[0:n, c, 0:DR]
                tt(rope_a[0:n, 0:DR], kr, kr, ALU.mult)
                dve.drain()
                dve.tensor_reduce(ss[0:n, 12:13], rope_a[0:n, 0:DR], X_AXIS, ALU.add)
                dve.wait_ge(S("k_sq"), i + 1)
                dve.tensor_reduce(s8[0:n, 1, :], sqs[0:n, 1, 0:512].rearrange("p (h d) -> p h d", h=H), X_AXIS, ALU.add)
                dve.drain()
                ts(s8[0:n, 1, :], s8[0:n, 1, :], ss[0:n, 12:13], None, ALU.add).then_inc(S("k_ss"), 1)

            def k_norm(i):
                c = ORDER[i]
                dve.wait_ge(S("k_r"), i + 1)
                if i:
                    kr = ckv[:, c, 0:DR]
                    k = kt[c].rearrange("p (h d) -> p h d", h=H)
                    tt(k[:, :, 0:DN], PS[(6, 0)[i - 1]][:, :].rearrange("p (h d) -> p h d", h=H), bc(r8[:, 1, :], [128, H, DN], 2), ALU.mult)
                    tt(k[:, :, DN:DQ], bc(kr, [128, H, DR], 1), bc(r8[:, 1, :], [128, H, DR], 2), ALU.mult)
                    dve.drain()
                dve.engine_nop().then_inc(S("k_done"), 1)

            gated(0)
            dve.wait_ge(S("ql_T"), 1)
            dve.tensor_copy(ckvT[:, :, 0:SEQ].rearrange("p l (c x) -> p c l x", c=2),
                            PS[2][:, :].rearrange("p (c l x) -> p c l x", c=2, l=2)).then_inc(S("latT"), 1)
            dve.tensor_copy(ckvT[:, :, SEQ:T], PS[3][:, 0:256].rearrange("p (l x) -> p l x", l=2)[:, :, 0:NS]).then_inc(S("latT"), 1)
            dve.tensor_copy(krn[:], PS[3][:, 256:256 + NS]).then_inc(S("latT"), 1)
            for i, c in enumerate(ORDER):
                r, n = CHUNKS[c]
                dve.wait_ge(S("ql_T"), i + 1)
                src = PS[3][:, 320:512] if c == 2 else PS[4 + c][:, 0:384]
                tt(qlT[:, :, r:r + n], src.rearrange("p (j x) -> p j x", j=3),
                   bc(g_ql[:], [128, 3, n], 2), ALU.mult).then_inc(S("qlT"), 1)
            q_rotate(0)
            gated(1)
            q_norm(0)
            k_sums(0)
            gated(2)
            k_norm(0)
            q_rotate(1)
            q_norm(1)
            dve.wait_ge(S("qs_T"), 1)
            for s2 in range(2):
                ps = slice(64 * s2, 64 * s2 + 64)
                dve.tensor_copy(qsT[ps, :, 64 * s2:64 * s2 + 64], PS[3][ps, 0:256].rearrange("p (a b) -> p a b", a=4))
            dve.tensor_copy(qrT[0:DR, :].rearrange("p (s h q) -> p h s q", s=8, h=8),
                            PS[2][0:DR, :].rearrange("p (h s q) -> p h s q", s=8, h=8))
            dve.drain()
            dve.engine_nop().then_inc(S("qsT"), 1)
            gated(3)
            dve.wait_ge(S("q_abs"), 1)
            for l in range(2):
                dve.tensor_copy(qabs[:, l, :].rearrange("p (s h q) -> p h s q", s=8, h=8),
                                PS[2 + l][:, :].rearrange("p (h s q) -> p h s q", s=8, h=8)).then_inc(S("qabs"), 1)
            k_sums(1)
            dve.wait_ge(S("s_new"), 1)
            tt(snew[0:NS].rearrange("p (s h q) -> p s h q", s=8, h=8), PS[2][0:NS, :].rearrange("p (s h q) -> p s h q", s=8, h=8),
               r8[0:NS, 2, :].unsqueeze(1).unsqueeze(3).broadcast_to([NS, 8, 8, 8]), ALU.mult).then_inc(S("snew"), 1)
            k_norm(1)
            q_rotate(2)
            q_norm(2)
            k_sums(2)
            k_norm(2)
            for b in range(8):
                c, hb, dst = b // 4, b % 2, (kT, qT)[b // 2 % 2]
                dve.wait_ge(S("heads_T"), b + 1)
                dve.tensor_copy(dst[0:DQ, 4 * hb:4 * hb + 4, 128 * c:128 * c + 128],
                                PS[(2, 3, 6, 7)[b % 4]][0:DQ, :].rearrange("p (a b) -> p a b", a=4)).then_inc(S("heads_ev"), 1)

            def scale_half(n, t, half):
                dve.wait_ge(S("rk"), 2 * n + half + 1)
                dve.wait_ge(S("scores"), n * PAGES + 4 * half + 4)
                src = PS[4 + half][:, :].rearrange("p (b c) -> p b c", b=4)[:, :, 64 * t:64 * t + 64]
                tt(s_all[t][:, 4 * half:4 * half + 4, :].rearrange("p b (h q) -> p b h q", h=H),
                   src.rearrange("p b (h q) -> p b h q", h=H),
                   bc(r8[:, 4 * half:4 * half + 4, :], [128, 4, H, DEC_T], 3), ALU.mult).then_inc(S("s_half"), 1)

            def maxima(n, t):
                scale_half(n, t, 1)
                dve.drain()
                dve.tensor_reduce(m1[:, 0:64], s_all[t].rearrange("p b c -> p c b"), X_AXIS, ALU.max)
                dve.drain()
                tt(m1[0:NS, 0:64], m1[0:NS, 0:64], snew[0:NS, bass.ds(n * 64, 64)], ALU.max).then_inc(S("m_part"), 1)

            def diagonal(n):
                dve.wait_ge(S("m_T"), n + 1)
                dve.tensor_reduce(mx[0:64, 0:1], PS[6][0:64, 0:128], X_AXIS, ALU.max)
                dve.drain()
                ts(dg[0:64, 0:64], ident[0:64, 0:64], mx[0:64, 0:1]).then_inc(S("m_diag"), 1)

            def subtract(n, t):
                dve.wait_ge(S("m_all"), n + 1)
                tt(s_all[t], s_all[t], bc(PS[6][:, 128:192], [128, PAGES, 64], 1), ALU.subtract)
                tt(pn[0:NS, :], snew[0:NS, bass.ds(n * 64, 64)], PS[6][0:NS, 128:192], ALU.subtract).then_inc(S("s_sub"), 1)

            def normalise(n):
                dve.wait_ge(S("ck_used"), n + 1)
                dve.reciprocal(rden[0:64, 0:1], PS[7][0:64, 0:1])
                dve.drain()
                ts(ocn[0:64], PS[7][0:64, 4:260], rden[0:64, 0:1]).then_inc(S("oc_n"), 1)

            def keep(n):
                dve.wait_ge(S("oc_T"), n + 1)
                dst = ocT.rearrange("p l (h x) -> p l h x", h=H)[:, :, :, bass.ds(n * DEC_T, DEC_T)]
                dve.tensor_copy(dst, PS[6][:, 256:512].rearrange("p (l x) -> p l x", l=2)[:, :, 0:64].rearrange("p l (h q) -> p l h q", h=H)).then_inc(S("ocT"), 1)

            def taps(j, part):
                for c in (2 * part, 2 * part + 1):
                    w = cw[:, bass.ds(j * CC + c, 1)]
                    dve.scalar_tensor_tensor(acc[:, c, 0:SEQ], glu[:, c, bass.ds(j, SEQ)], w, acc[:, c, 0:SEQ], ALU.mult, ALU.add)

            def sequence(n, t, first, chunk=None):
                for b in range(PAGES):
                    m = n * PAGES + b
                    dve.wait_ge(S("sq"), m + 1)
                    dve.tensor_reduce(s8[:, b, :], sqk[b % 2].rearrange("p (h d) -> p h d", h=H), X_AXIS, ALU.add).then_inc(S("kss"), 1)
                    if b % 4 == 3:
                        half = b // 4
                        if b == 3:
                            dve.wait_ge(S("sqr"), n + 1)
                            dve.tensor_reduce(rss[:], sqr[:], X_AXIS, ALU.add).then_inc(S("rss_done"), 1)
                        dve.drain()
                        h8 = s8[:, 4 * half:4 * half + 4, :]
                        tt(h8, h8, bc(rss[:, 4 * half:4 * half + 4], [128, 4, H], 2), ALU.add).then_inc(S("ss_half"), 1)
                    if b == 5:
                        scale_half(n, t, 0)
                    if not first:
                        if b == 0:
                            maxima(n - 1, 1 - t)
                        if b == 1:
                            diagonal(n - 1)
                        if b == 2:
                            subtract(n - 1, 1 - t)
                        if b == 5:
                            normalise(n - 1)
                        if b == 6:
                            keep(n - 1)
                    taps(4 * n + b // 2, b % 2)
                    if chunk is not None and b == 7:
                        dve.wait_ge(S("s_prod"), chunk + 1)
                        dve.tensor_reduce(acc[:, bass.ds(chunk, 1), SEQ:T].rearrange("p a b -> p (a b)"), s_prod,
                                          X_AXIS, ALU.add).then_inc(S("s_sum"), 1)
                    dve.drain()
            dve.wait_ge(S("snew_m"), 2)
            sequence(0, 0, True, 0)
            with dve.Fori(0, 3) as i:
                sequence(2 * i + 1, 1, False, i + 1)
                sequence(2 * i + 2, 0, False)
            sequence(7, 1, False)
            tt(acc[:, :, SEQ:T], acc[:, :, SEQ:T], bc(g_cb[:], [128, CC, NS], 2), ALU.add).then_inc(S("conv_done"), 1)
            maxima(7, 1)
            diagonal(7)
            subtract(7, 1)
            normalise(7)
            keep(7)

            def p_scores(h):
                dve.wait_ge(S("p_sc"), h + 1)
                if h >= 2:
                    dve.wait_ge(S("p_tr"), h - 1)
                tt(pr[h % 2], PS[h % 2][:, 0:384].rearrange("p (a b) -> p a b", a=3),
                   causal3.rearrange("p (a b) -> p a b", a=3), ALU.add).then_inc(S("p_s"), 1)
                dve.drain()
                dve.tensor_reduce(pm[:, h % 2, 0:1], pr[h % 2][:, 0, :], X_AXIS, ALU.max)
                dve.tensor_reduce(pm[:, h % 2, 1:2], pr[h % 2][:, 1:3, :], mybir.AxisListType.XY, ALU.max)
                dve.drain()
                ts(pm[:, h % 2, :], pm[:, h % 2, :], -SCALE).then_inc(S("p_m"), 1)

            def p_rows(h):
                dve.wait_ge(S("p_out"), h + 1)
                dve.reciprocal(rsm[:, h % 2, :], psm[:, h % 2, :])
                dve.drain()
                o = PS[4 + h % 2]
                for c in range(2):
                    last = ts(attn_t[:, c, DV * h:DV * h + DV], o[:, 128 * c:128 * c + DV], rsm[:, h % 2, c:c + 1])
                dve.drain()
                dve.engine_nop().then_inc(S("p_o"), 1)
            for h in range(H + 2):
                if h < H:
                    p_scores(h)
                if h >= 2:
                    p_rows(h - 2)
            dve.wait_ge(S("attn_s"), 1)
            dve.tensor_copy(attn_t[0:NS, 2, :], PS[7][0:NS, :]).then_inc(S("attn_done"), 1)
            for c in range(NC):
                dve.wait_ge(S("conv_T"), c + 1)
                dve.drain()
                dve.bn_stats(st6[:], PS[(6, 7, 3)[c]][:, :])
                dve.drain()
                last = dve.bn_aggr(mv[:, c, :], st6[:])
            last.then_inc(S("mv"), 1)
            dve.wait_ge(S("root"), 2)
            for c, (r, n) in enumerate(CHUNKS):
                ts(attn_t[0:n, c, :], attn_t[0:n, c, :], rs[0:n, c:c + 1]).then_inc(S("attn_n"), 1)
            dve.wait_ge(S("root"), 3)
            for c in range(NC):
                ts(conv_t[:, c, :], PS[(6, 7, 3)[c]][:, :], mv[:, c, 0:1], rs[:, 3 + c:4 + c], ALU.subtract, ALU.mult).then_inc(S("ln"), 1)
            dve.drain()
            dve.wait_ge(S("ln_in"), 32)
            tt(conv_t, conv_t, bc(lng, [128, NC, DC], 1), ALU.mult)
            dve.drain()
            tt(conv_t, conv_t, bc(lnb, [128, NC, DC], 1), ALU.add).then_inc(S("ln"), 1)

            def mix(i):
                kind, c = i // 3, i % 3
                r, n = CHUNKS[c]
                dve.wait_ge(S("mix_T"), i + 1)
                k = 4 if kind == 0 else 0
                tt(xT[:, k:k + 4, r:r + n], PS[(0, 1, 2, 6, 7, 6)[i]][:, :].rearrange("p (a b) -> p a b", a=4)[:, :, 0:n],
                   bc((g_oa if kind == 0 else g_oc)[:], [128, 4, n], 2), ALU.mult).then_inc(S("mixT"), 1)
            for i in range(3):
                mix(i)
            ez = view(R_C, NC, DC)
            dve.wait_ge(S("ez"), 1)
            ts(ez, ez, 1.0, None, ALU.add)
            dve.drain()
            dve.reciprocal(ez, ez)
            dve.drain()
            tt(conv_t, conv_t, ez, ALU.mult).then_inc(S("ln"), 1)
            dve.wait_ge(S("root"), 4)
            for c in range(NC):
                ts(conv_t[:, c, :], conv_t[:, c, :], rs[:, 6 + c:7 + c]).then_inc(S("conv_n"), 1)
            for i in range(3, 6):
                mix(i)
            for c, (r, n) in enumerate(CHUNKS):
                for hf in range(2):
                    dve.wait_ge(S("merged"), 2 * c + hf + 1)
                    xs = X[0:n, c, 512 * hf:512 * hf + 512]
                    last = tt(xs, xs, PS[(4, 0, 2)[c] + hf][0:n, :], ALU.add)
                dve.drain()
                dve.engine_nop().then_inc(S("h_rows"), 1)
            dve.wait_ge(S("root"), 5)
            for c, (r, n) in enumerate(CHUNKS):
                ts(xn2[0:n, c, :], X[0:n, c, :], rs[0:n, 9 + c:10 + c]).then_inc(S("xn2"), 1)
            for g in range(6):
                c, (r, n) = g // 2, CHUNKS[g // 2]
                k = 4 * (g % 2)
                dve.wait_ge(S("h_T"), g + 1)
                tt(xT[:, k:k + 4, r:r + n], PS[(0, 1, 4, 5, 6, 7)[g]][:, :].rearrange("p (a b) -> p a b", a=4)[:, :, 0:n],
                   bc(g_ffn[:, k:k + 4], [128, 4, n], 2), ALU.mult).then_inc(S("hT"), 1)
            dve.wait_ge(S("route_mm"), 1)
            dve.wait_ge(S("moe_zero"), 1)
            dve.tensor_copy(lgT[:, 0:T], PS[2][0:NE, 0:T]).then_inc(S("lgT"), 1)
            dve.wait_ge(S("route_mm"), 2)
            tt(lg[:], PS[3][:, 0:NC * NE].rearrange("p (c e) -> p c e", c=NC), bc(br[:], [128, NC, NE], 1), ALU.add)
            dve.drain()
            for c in range(NC):
                dve.max(v8[:, c, :], lg[:, c, :])
            dve.drain()
            for c in range(NC):
                dve.max_index(i8[:, c, :], v8[:, c, :], lg[:, c, :])
            tt(gate4[:], v8[:, :, 0:TOPK], v8[:, :, 0:1].broadcast_to([128, NC, TOPK]), ALU.subtract).then_inc(S("gate_d"), 1)
            dve.drain()
            dve.tensor_copy(i8f[:], i8[:])
            dve.memset(M[:], 0.0)
            dve.memset(G[:], 0.0)
            dve.wait_ge(S("gate_e"), 1)
            dve.tensor_reduce(gsum[:], gate4[:], X_AXIS, ALU.add)
            dve.drain()
            dve.reciprocal(gsum[:], gsum[:])
            dve.drain()
            tt(gate4[:], gate4[:], bc(gsum[:], [128, NC, TOPK], 2), ALU.mult)
            dve.drain()
            full = [128, NC, NE]
            for k in range(TOPK):
                tt(eq[:], bc(iota[:, 0:NE], full, 1), i8f[:, :, k:k + 1].broadcast_to(full), ALU.is_equal)
                dve.drain()
                tt(M[:], M[:], eq[:], ALU.add)
                dve.drain()
                tt(eq[:], eq[:], gate4[:, :, k:k + 1].broadcast_to(full), ALU.mult)
                dve.drain()
                tt(G[:], G[:], eq[:], ALU.add)
                dve.drain()
            dve.memset(M[NS:128, 2, :], 0.0)
            dve.memset(G[NS:128, 2, :], 0.0)
            dve.drain()
            dve.engine_nop().then_inc(S("routed"), 1)
            dve.wait_ge(S("moe_zero"), 1)
            dve.wait_ge(S("route_mm"), 3)
            first = posI[:, :, 0:NE]
            dve.scalar_tensor_tensor(first, PS[0][:, 0:NC * NE].rearrange("p (c e) -> p c e", c=NC), BIG, M[:], ALU.add, ALU.mult)
            dve.tensor_copy(gateI[:, :, 0:NE], G[:])
            cnt = PS[1][0:NE, 0:128]
            ts(extra[:], cnt, float(SLOTS), None, ALU.is_gt)
            for b in range(2, T // SLOTS):
                dve.drain()
                dve.scalar_tensor_tensor(extra[:], cnt, float(SLOTS * b), extra[:], ALU.is_gt, ALU.add)
            dve.drain()
            ts(first, first, -BIG, None, ALU.add)
            dve.drain()
            dve.engine_nop().then_inc(S("routed"), 1)
            dve.wait_ge(S("route_mm"), 4)
            tt(rel[:], iota[0:NE, :], PS[2][0:NE, 0:64], ALU.subtract)
            dve.drain()
            ts(P[:], rel[:], 0.0, None, ALU.is_ge)
            tt(tmpP[:], rel[:], extra[:, 0:64], ALU.is_lt)
            dve.drain()
            tt(P[:], P[:], tmpP[:], ALU.mult)
            ts(rel[:], rel[:], -float(SLOTS), BIG - SLOTS, ALU.mult, ALU.add)
            dve.drain()
            tt(tmpP[:], rel[:], P[:], ALU.mult)
            ts(tab_f[0:1, 66:80], iota[0:1, 0:14], 2.0)
            dve.drain()
            tt(tab_f[0:1, 66:80], tab_f[0:1, 66:80], PS[4][0:1, 0:14], ALU.is_lt)
            dve.drain()
            dve.tensor_reduce(tab_f[0:1, 0:1], tab_f[0:1, 66:80], X_AXIS, ALU.add).then_inc(S("routed"), 1)
            dve.drain()
            ts(tab_f[0:1, 0:1], tab_f[0:1, 0:1], float(NE // 2), None, ALU.add)
            dve.wait_ge(S("route_mm"), 5)
            dve.tensor_copy(posT[:], PS[5][0:NE, 0:384])
            dve.tensor_copy(GT[0:NE, :], PS[6][0:NE, 0:384])
            dve.drain()
            dve.engine_nop().then_inc(S("routed"), 1)
            dve.wait_ge(S("route_mm"), 6)
            dve.tensor_copy(tab_f[0:1, 1:65], PS[4][0:1, 128:192])
            dve.drain()
            dve.tensor_copy(tab[0:1, 0:65], tab_f[0:1, 0:65]).then_inc(S("table"), 1)
            ts(posI[:, :, NE:ITEMS], PS[7][:, 0:192].rearrange("p (c i) -> p c i", c=NC), -BIG, None, ALU.add)
            dve.tensor_copy(gateI[:, :, NE:ITEMS], PS[3][:, 0:192].rearrange("p (c i) -> p c i", c=NC))
            dve.drain()
            dve.engine_nop().then_inc(S("tab_ev"), 1)
            for q in range(6):
                dve.wait_ge(S("y_bias"), q + 1)
                xs = X[:, q // 2, 512 * (q % 2):512 * (q % 2) + 512]
                tt(xs, xs, PS[q % 2][:, :], ALU.add).then_inc(S("ybias"), 1)

            gsb_, usb_, sgb_, hsb, hT = gsb

            def select(i):
                for t in range(2):
                    pos = posI[:, :, bass.ds(2 * i + t, 1)].broadcast_to([128, NC, SLOTS])
                    last = tt(sel[:, :, 64 * t:64 * t + 64], bc(iota, [128, NC, SLOTS], 1), pos, ALU.is_equal)
                dve.drain()
                dve.engine_nop().then_inc(S("sel"), 1)

            def select_gates(i):
                for c in range(NC):
                    pos = [posI[:, c, bass.ds(2 * i + t, 1)] for t in range(2)]
                    gat = [gateI[:, c, bass.ds(2 * i + t, 1)] for t in range(2)]
                    for k in range(3):
                        dve.tensor_scalar(selg[:, c, 64 * k:64 * k + 64], iota, pos[k % 2], gat[k % 2], ALU.is_equal, ALU.mult)
                dve.drain()
                dve.engine_nop().then_inc(S("selg"), 1)

            def take_tokens(v):
                dve.wait_ge(S("gathered"), v)
                for j in range(2):
                    tt(xg[:, 4 * j:4 * j + 4, :], PS[5 + j][:, :].rearrange("p (a b) -> p a b", a=4),
                       bc(g_ffn[:, 4 * j:4 * j + 4], [128, 4, 128], 2), ALU.mult)
                dve.drain()
                dve.engine_nop().then_inc(S("xg"), 1)

            def swiglu(i, t):
                dve.wait_ge(S("gu_done"), 2 * i + t + 1)
                ts(gsb_, PS[0][:, :], LIMIT, None, ALU.min).then_inc(S("g_min"), 1)
                ts(usb_, PS[1][:, :], -LIMIT, LIMIT, ALU.max, ALU.min).then_inc(S("gu_ev"), 1)
                dve.drain()
                dve.scalar_tensor_tensor(usb_, usb_, 1.0, gsb_, ALU.add, ALU.mult)
                dve.drain()
                dve.wait_ge(S("sig"), 2 * i + t + 1)
                tt(hsb, usb_, sgb_, ALU.mult).then_inc(S("h"), 1)

            def add_rows(v):
                for q in range(6):
                    dve.wait_ge(S("combined"), 6 * v + q + 1)
                    xs = X[:, q // 2, 512 * (q % 2):512 * (q % 2) + 512]
                    tt(xs, xs, PS[5 + q % 3][:, :], ALU.add).then_inc(S("y_add"), 1)

            dve.engine_nop().then_inc(S("gu_ev"), 1)
            select(0)
            select_gates(0)
            take_tokens(1)
            n_iter = dve.value_load(tab[0:1, 0:1], min_val=NE // 2, max_val=MAX_ITER)
            with dve.Fori(0, n_iter) as i:
                dve.wait_ge(S("gathered"), i + 1)
                select(i + 1)
                swiglu(i, 0)
                add_rows(i)
                swiglu(i, 1)
                dve.wait_ge(S("sel_T"), i + 1)
                select_gates(i + 1)
                take_tokens(i + 2)
            add_rows(n_iter)
            dve.drain()
            dve.engine_nop().then_inc(S("y_done"), 1)


_INS = ["x_prompt", "x_sample", "cache_kv_latent", "cache_k_rope", "state_conv", "page_table", "norm_mix", "w_in",
        "norm_q_lat", "w_uq", "norm_kv_lat", "w_ukv", "norm_qk_q", "norm_qk_k", "conv_w", "conv_b", "conv_ln_g",
        "conv_ln_b", "norm_out_conv", "norm_out_attn", "w_out", "norm_ffn", "w_router", "b_router", "w_gate_up",
        "b_gate_up", "w_down", "b_down"]
_OUTS = [(1, SEQ, D), (DEC_B, DEC_T, D), (1, 1, SEQ, KVL), (1, 1, SEQ, DR), (1, 1, W - 1, DC),
         (1, DEC_B, DEC_T, KVL), (1, DEC_B, DEC_T, DR), (1, DEC_B, W - 1, DC)]


def _constants():
    import numpy as np

    f = np.float32
    i = np.arange(128)
    pack = np.zeros((128, C_W), f)
    pack[:, C_ID:C_ID + 128] = np.eye(128, dtype=f)
    pack[:, C_UP:C_UP + 128] = i[:, None] < i[None, :]
    pack[:, C_ONE:C_ONE + 128] = 1
    later = np.where(i[None, :] <= i[:, None], f(0), f(-1e30))
    pack[:, C_CAUS:C_CAUS + 128] = later
    pack[:, C_CAUS + 256:C_CAUS + 384] = later
    pack[:, C_IOTA:C_IOTA + 64] = np.arange(64)
    pack[:, C_PIDX] = i
    pack[:, C_EPS] = EPS
    pack[0, C_ONE0:C_ONE0 + 64] = 1
    pos = np.zeros(NC * 128, f)
    pos[:SEQ] = np.arange(SEQ)
    pos[SEQ:T] = np.tile(PAGE * PAGES + np.arange(DEC_T), DEC_B)
    freq = f(10000.0) ** (-np.arange(16, dtype=f) / f(16))
    ang = pos[:, None] * freq[None, :]
    tabs = [np.ascontiguousarray(t(ang).reshape(NC, 128, 16).transpose(1, 0, 2)).astype(f) for t in (np.cos, np.sin)]
    return {"pack": pack, "cos": tabs[0], "sin": tabs[1]}


def kernel(**inputs):
    import numpy as _np
    import concourse.bacc as _bacc
    from concourse import mybir as _mybir
    from concourse.bass_utils import run_bass_kernel_spmd as _run

    nc = _bacc.Bacc("TRN2", target_bir_lowering=False, num_devices=1)
    arrays, args = {}, []
    for name in _INS:
        a = _np.ascontiguousarray(inputs[name])
        arrays[f"in_{name}_dram"] = a
        args.append(nc.dram_tensor(f"in_{name}_dram", a.shape, _mybir.dt.from_np(a.dtype), kind="ExternalInput").ap())
    consts = []
    for name, a in _constants().items():
        arrays[f"const_{name}_dram"] = a
        consts.append(nc.dram_tensor(f"const_{name}_dram", a.shape, _mybir.dt.float32, kind="ExternalInput").ap())
    outs = [nc.dram_tensor(f"out_{i}_dram", s, _mybir.dt.float32, kind="ExternalOutput").ap() for i, s in enumerate(_OUTS)]
    decoder_layer(nc, args, consts, outs)
    r = _run(nc, [arrays], core_ids=[0])
    return tuple(r.results[0][f"out_{i}_dram"] for i in range(len(_OUTS)))
```

```python
import concourse.bass as bass
from concourse import mybir
from concourse.alu_op_type import AluOpType as ALU
from contextlib import ExitStack

F32 = mybir.dt.float32
I32 = mybir.dt.int32
U32 = mybir.dt.uint32
ACT = mybir.ActivationFunctionType
X_AXIS = mybir.AxisListType.X

D = 1024
KD = D // 128
SEQ, DEC_B, DEC_T = 256, 8, 8
NS = DEC_B * DEC_T
T = SEQ + NS
CHUNKS = [(0, 128), (128, 128), (256, NS)]
ORDER = (2, 0, 1)
NC = len(CHUNKS)
DC = 512
CC = DC // 128
W = 31
H, DN, DR, DV = 8, 64, 32, 64
DQ = DN + DR
QL, KVL = 384, 256
D_IN = 2 * DC + QL + KVL + DR
PAGE, PAGES = 128, 8
POOL_PAGES = 81
NE, TOPK = 32, 4
DE = 1024
LIMIT, ALPHA = 7.0, 1.702
EPS = 1e-6
SCALE = DQ ** -0.5
BIG = 4096.0
SLOTS = 64
OVER = 20
ITEMS = 64
EXTRA_AT = NE // 2
TAB_ST, TAB_E, TAB_W = 1, 64, 128
MAX_ITER = (NE + OVER) // 2

ONE, LAT = DR, DR + 4
CROW = LAT + KVL
SEG = W + DEC_T
SEG0 = W - 1 + SEQ
GLU_W = SEG0 + DEC_B * SEG
C_ID, C_UP, C_ONE, C_CAUS, C_IOTA, C_PIDX, C_EPS, C_ONE0 = 0, 128, 256, 384, 768, 832, 833, 834
C_W = 834 + 64

R_GU, R_DN = 0, 16384
R_X = R_DN + 8192
R_W = R_X + 3072
R_M = R_W + 13568
ARENA_W = R_M + 8544
PARTS = [R_GU, R_GU + 8192, R_DN, ARENA_W - 8192]


def decoder_layer(nc, ins, consts, outs):
    (x_prompt, x_sample, cache_kv, cache_kr, state_conv, page_table, norm_mix, w_in, norm_q_lat,
     w_uq, norm_kv_lat, w_ukv, norm_qk_q, norm_qk_k, conv_w, conv_b, conv_ln_g, conv_ln_b,
     norm_out_conv, norm_out_attn, w_out, norm_ffn, w_router, b_router, w_gate_up, b_gate_up,
     w_down, b_down) = ins
    c_pack, c_cos, c_sin, c_odd = consts
    y_p, y_s, lat_p, rope_p, conv_p, lat_s, rope_s, conv_s = outs

    ctx = ExitStack()
    with ctx:
        sb = ctx.enter_context(nc.sbuf_tensor("arena", [128, ARENA_W], F32))

        def view(off, *dims, rows=128):
            n = 1
            for d in dims:
                n *= d
            v = sb[0:rows, off:off + n]
            if len(dims) == 2:
                v = v.rearrange("p (a b) -> p a b", a=dims[0])
            if len(dims) == 3:
                v = v.rearrange("p (a b c) -> p a b c", a=dims[0], b=dims[1])
            return v

        def own(name, shape, dt=F32):
            return ctx.enter_context(nc.sbuf_tensor(name, shape, dt))

        parts = PARTS
        dn_w = view(parts[2], KD, D)
        X = view(R_X, NC, D)
        o = R_GU

        def take(n):
            nonlocal o
            o += n
            return o - n
        ql = view(take(NC * QL), NC, QL)
        ckvT = view(take(2 * T), 2, T)
        qlT = view(take(3 * T), 3, T)
        s_prod = view(o, 64, W)
        eg = view(take(2 * T), 2, T)
        sqs = view(take(2 * 768), 2, 768)
        qsn = view(take(512), 512)
        qsr = view(take(352), 352)
        qsT = view(take(4 * 128), 4, 2 * NS)
        snew = view(take(512), 512)
        wkT = view(take(4 * KVL), 4, KVL)
        R_U = take(2304)
        wuq = view(R_U, 3, 768)
        s_all = [view(R_U + 512 * i, PAGES, 64) for i in range(2)]
        sqk = [view(R_U + 1024 + 512 * i, 512) for i in range(2)]
        pr = [view(R_U + 384 * i, 3, 128) for i in range(2)]
        pT = [view(R_U + 768 + 384 * i, 3, 128) for i in range(2)]
        qt = [view(o + 768 * i, 768) for i in range(3)]
        st_rows = view(take(2 * DC), 2, DC)[0:120]
        rows1 = view(take(128), 128)[0:W * CC]
        rows2 = view(take(128), 128)[0:31]
        row_out = view(take(DC), DC)[0:NS]
        row_out2 = view(take(DC), DC)[0:32]
        gpk = view(take(CC * NS), CC, NS)
        sqr = view(take(PAGES * DR), PAGES, DR)
        ocn = view(take(KVL), KVL)
        gkv = view(take(KVL), KVL)
        gqk = view(take(DQ), DQ)
        gkk = view(take(DQ), DQ)
        cos = view(take(NC * 16), NC, 16)
        sin = view(take(NC * 16), NC, 16)
        rope_a = view(take(128), 128)
        rope_b = view(take(128), 128)
        ckv = view(take(NC * CROW), NC, CROW)
        assert o <= R_DN, o
        o = R_DN
        qT = view(take(H * SEQ), H, SEQ)
        kT = view(take(H * SEQ), H, SEQ)
        vt = view(take(2 * 576), 2, 576)
        qabs = view(take(2 * 512), 2, 512)
        kt = [view(o + 768 * i, 768) for i in range(2)]
        ocT = view(take(2 * 512), 2, 512)
        cT = view(take(2 * 384), 2, 384)
        assert o <= R_X
        win = view(R_W, KD, D_IN)
        wout = view(R_W, KD, D)
        ck = [view(R_W + 8192 + i * PAGES * CROW, PAGES, CROW) for i in range(2)]
        lng = view(R_W + 8192, DC)
        lnb = view(R_W + 8192 + 512, DC)
        conv_t = view(R_W + 8192 + 1024, NC, DC)
        attn_t = view(R_W + 8192 + 2560, NC, DC)
        assert 8192 + 2560 + 1536 <= 13568
        o = R_W
        xn2 = view(take(NC * D), NC, D)
        xg = view(take(KD * 128), KD, 128)
        ysb = view(take(2 * 512), 2, 512)
        sel = view(take(NC * 128), NC, 128)
        selg = view(take(NC * 192), NC, 192)
        selT = view(take(2 * NC * 128), 2, NC * 128)
        posI = view(take(NC * ITEMS), NC, ITEMS)
        gateI = view(take(NC * ITEMS), NC, ITEMS)
        bias = view(take(2 * DE), 2 * DE)
        gsb = [view(take(512), 512) for _ in range(5)]
        assert o <= R_M
        o = R_M
        xT = view(take(KD * T), KD, T)
        wk = view(take(2 * 512), 2, 512)
        wv = view(take(2 * 512), 2, 512)
        R_C = take(CC * GLU_W)
        glu = view(R_C, CC, GLU_W)
        acc = view(take(CC * 384), CC, 384)
        xn = view(R_C, NC, D)
        ez = view(R_C, NC, DC)
        scr = view(R_C, NC * DC)
        bdn = view(R_M + KD * T, D)
        assert take(0) - R_M <= 8544, take(0) - R_M
        o = R_C + 3 * 512
        lgT = view(take(384), 384)[0:NE]
        GT = view(take(384), 384)
        R_Z, posT_all = o, view(take(384), 384)
        extra_all = view(take(128), 128)
        wide = [view(o + 64 * i, 128) for i in range(3)]
        P, tmpP, begun, before = (view(take(64), 64)[0:NE] for _ in range(4))
        zero_rows = view(R_Z, o - R_Z)
        posT, extra = posT_all[0:NE], extra_all[0:NE]
        lg, M, G = (view(take(NC * NE), NC, NE) for _ in range(3))
        eq = view(take(NC * TOPK * NE), NC, TOPK * NE).rearrange("p c (k e) -> p c k e", k=TOPK)
        assert o <= R_M + 8544, o

        cst = own("cst", [128, C_W])
        ident = cst[:, C_ID:C_ID + 128]
        upper = cst[:, C_UP:C_UP + 128]
        ones = cst[:, C_ONE:C_ONE + 128]
        causal3 = cst[:, C_CAUS:C_CAUS + 384]
        iota = cst[:, C_IOTA:C_IOTA + 64]
        pidx = cst[:, C_PIDX:C_PIDX + 1]
        eps = cst[:, C_EPS:C_EPS + 1]
        one_row = cst[:, C_ONE0:C_ONE0 + 64]
        cw = own("cw", [128, 32 * CC])
        gc = own("gc", [128, 31])
        g_mix, g_ql, g_cb, g_oc, g_oa, g_ffn = (gc[:, a:b] for a, b in
                                                ((0, 8), (8, 11), (11, 15), (15, 19), (19, 23), (23, 31)))
        ss = own("ss", [128, 16])
        rs = own("rs", [128, 16])
        lnx = own("lnx", [128, 64])
        s8 = own("s8", [128, PAGES, H])
        r8 = own("r8", [128, PAGES, H])
        rss = own("rss", [128, PAGES])
        m1 = own("m1", [128, 128])
        mx = own("mx", [128, 2])
        dg = own("dg", [128, 128])
        pn = own("pn", [128, 64])
        rden = own("rden", [128, 2])
        pt_sb = own("pt_sb", [1, DEC_B * PAGES], I32)
        qrT = own("qrT", [128, 512])
        krn = own("krn", [128, NS])
        pm = own("pm", [128, 2, 2])
        psm = own("psm", [128, 2, 2])
        rsm = own("rsm", [128, 2, 2])
        wr = own("wr", [128, KD, NE])
        br = own("br", [128, NE])
        v8 = own("v8", [128, NC, 8])
        i8 = own("i8", [128, NC, 8], U32)
        i8f = own("i8f", [128, NC, 8])
        gate4 = own("gate4", [128, NC, TOPK])
        gsum = own("gsum", [128, NC])
        tab_f = own("tab_f", [1, TAB_W])
        tab = own("tab", [1, TAB_W], I32)
        odd_tab = own("odd_tab", [1, NE], I32)
        st6 = own("st6", [128, 6])
        mv = own("mv", [128, NC, 2])

        PS = [ctx.enter_context(nc.psum_tensor(f"bank{i}", [128, 512], F32)) for i in range(8)]

        sems = {}

        def S(name):
            if name not in sems:
                sems[name] = ctx.enter_context(nc.semaphore(name))
            return sems[name]

        def bc(ap, shape, axis):
            return ap.unsqueeze(axis).broadcast_to(shape)

        def page_count(n, t):
            return (n - t) * (8 * PAGES) + 16 * PAGES

        def windows(c):
            v = glu[:, bass.ds(c, 1), SEG0:GLU_W].rearrange("p c (s u) -> p (c s) u", u=SEG)[:, :, 0:DEC_T]
            return bass.AP(v.tensor, v.offset, [list(d) for d in v.ap] + [[1, W]])

        block = ctx.enter_context(nc.Block())

        @block.sync
        def _(sp):
            sp.dma_start(X[:, 0:2, :], x_prompt[0].rearrange("(c p) d -> p c d", p=128)).then_inc(S("x_in"), 16)
            sp.dma_start(X[0:NS, 2, :], x_sample.rearrange("b t d -> (b t) d")).then_inc(S("x_in"), 16)
            sp.dma_start(gkv[:], norm_kv_lat[0:1].partition_broadcast(128)).then_inc(S("g_in"), 16)
            for g, src in ((gqk, norm_qk_q), (gkk, norm_qk_k)):
                sp.dma_start(g[:, 0:80], src[0:1].partition_broadcast(128)).then_inc(S("g_in"), 16)
                sp.dma_start(g[:, 80:96], src[0:1, 64:80].partition_broadcast(128)).then_inc(S("g_in"), 16)
            for i in range(2):
                sp.dma_start(st_rows[:, i, :], state_conv[0, 4 * i:4 * i + 4].rearrange("b t c -> (b t) c")).then_inc(S("st_in"), 16)
            sp.wait_ge(S("rows_in"), 16 * 7)
            for cols, arrived in ((slice(2 * DC, D_IN), "win_in"), (slice(0, 2 * DC), "winc_in")):
                for kk in range(2):
                    sp.dma_start(win[:, 4 * kk:4 * kk + 4, cols],
                                 w_in[0, 512 * kk:512 * kk + 512, cols].rearrange("(k p) n -> p k n", p=128)).then_inc(S(arrived), 16)
            w4 = w_ukv[0].rearrange("(l p) h d -> l p h d", p=128)
            for l in range(2):
                sp.dma_start(wk[:, l, :].rearrange("p (h d) -> p h d", h=H), w4[l][:, :, 0:DN]).then_inc(S("wkv_in"), 16)
                sp.dma_start(wv[:, l, :].rearrange("p (h d) -> p h d", h=H), w4[l][:, :, DN:128]).then_inc(S("wkv_in"), 16)
            sp.dma_start(wuq, w_uq[0].rearrange("(k p) h d -> p k (h d)", p=128)).then_inc(S("wuq_in"), 16)

            def load_pages(n, t, first):
                pages = [sp.value_load(pt_sb[0:1, bass.ds(n * PAGES + j, 1)], min_val=0, max_val=POOL_PAGES - 1)
                         for j in range(PAGES)]
                if not first:
                    sp.wait_ge(S("ck_used"), n - 1)
                for j, page in enumerate(pages):
                    arrived = S(f"ck_in{t}" if j < PAGES // 2 else f"ck2_in{t}")
                    sp.dma_start(ck[t][:, j, LAT:CROW],
                                 cache_kv[0, bass.ds(page, 1)].rearrange("a p c -> p (a c)")).then_inc(arrived, 16)
                    sp.dma_start(ck[t][:, j, 0:DR],
                                 cache_kr[0, bass.ds(page, 1)].rearrange("a p c -> p (a c)")).then_inc(arrived, 16)

            sp.wait_ge(S("pt_in"), 16)
            sp.wait_ge(S("proj_done"), 3 + 2 * CC)
            load_pages(0, 0, True)
            load_pages(1, 1, True)
            sp.dma_start(wout, w_out[0].rearrange("(k p) n -> p k n", p=128)).then_inc(S("wout_in"), 16)

            def weights(e, g, u):
                at = parts[3 if g == 0 and e[1] else g] + 4096 * u
                dst = sb[:, at:at + 4096]
                if g < 2:
                    rows = 512 * g + 256 * u
                    src = w_gate_up[0, bass.ds(e[0], 1), rows:rows + 256]
                    arrived = f"gu_odd{u}" if g == 0 and e[1] else f"gu_in{2 * g + u}"
                else:
                    src = w_down[0, bass.ds(e[0], 1), 512 * u:512 * u + 512]
                    arrived = f"dn_in{u}"
                k = 2 if g < 2 else 4
                sp.dma_start(dst.rearrange("p (k n) -> p k n", k=k), src.rearrange("a (k p) n -> p k (a n)", p=128)).then_inc(S(arrived), 16)

            def bias_row(e):
                sp.dma_start(bias[0:1, :], b_gate_up[0, bass.ds(e[0], 1), :]).then_inc(S("bias_in"), 16)

            with sp.Fori(1, 4) as i:
                load_pages(2 * i, 0, False)
                load_pages(2 * i + 1, 1, False)
            sp.wait_ge(S("ck_used"), DEC_B)
            sp.dma_start(lng, conv_ln_g[0:1].partition_broadcast(128)).then_inc(S("ln_in"), 16)
            sp.dma_start(lnb, conv_ln_b[0:1].partition_broadcast(128)).then_inc(S("ln_in"), 16)

            sp.wait_ge(S("attn_rows"), 2)
            sp.wait_ge(S("out"), 16 * 14)
            for g in range(3):
                for u in range(2):
                    weights((0, 0), g, u)
            sp.wait_ge(S("moe_zero"), 2)
            bias_row((0, 0))

            used = ["gu_used0", "gu_used1", "gu_used2", "gu_done", "dn_used0", "dn_done"]

            def first_item(e):
                return sp.value_load(tab[0:1, bass.ds(e + TAB_ST, 1)], min_val=0, max_val=ITEMS - 1)

            def part0(e):
                begin = first_item(e[0] - 1)
                for u in range(2):
                    sp.wait_ge(S(used[u]), begin)
                    weights(e, 0, u)

            def expert(e, other, ahead):
                begin, before_ = first_item(e[0]), first_item(e[0] - 1)
                if ahead:
                    before2 = first_item(e[0] - 2)
                    with sp.If(before_ < before2 + 2):
                        part0(e)
                if other is not None:
                    with sp.If(begin > before_ + 1):
                        part0(other)
                sp.wait_ge(S("bias_used"), begin)
                bias_row(e)
                for g in (1, 2):
                    for u in range(2):
                        sp.wait_ge(S(used[2 * g + u]), begin)
                        weights(e, g, u)
            sp.wait_ge(S("table"), 1)
            sp.wait_ge(S("ybias"), 6)
            weights((1, 1), 0, 0)
            weights((1, 1), 0, 1)
            expert((1, 1), (2, 0), False)
            with sp.Fori(1, NE // 2 - 1) as i:
                expert((2 * i, 0), (2 * i + 1, 1), True)
                expert((2 * i + 1, 1), (2 * i + 2, 0), True)
            expert((NE - 2, 0), (NE - 1, 1), True)
            expert((NE - 1, 1), None, True)
            sp.wait_ge(S("y_done"), 1)
            sp.dma_start(y_p[0].rearrange("(c p) d -> p c d", p=128), X[:, 0:2, :]).then_inc(S("y_out"), 16)
            sp.dma_start(y_s.rearrange("b t d -> (b t) d"), X[0:NS, 2, :]).then_inc(S("y_out"), 16)
            sp.wait_ge(S("y_out"), 32)

        @block.gpsimd
        def _(pool):
            pool.dma_start(pt_sb[:], page_table.rearrange("(a b) p -> a (b p)", a=1)).then_inc(S("pt_in"), 16)
            pool.dma_start(odd_tab[:], c_odd).then_inc(S("odd_in"), 16)
            for t in (ss, rs):
                pool.memset(t[:], 0.0)
            pool.memset(cw[:, W * CC:32 * CC], 0.0).then_inc(S("zeroed"), 1)
            for t in (m1, dg, pn, qrT):
                pool.memset(t[:], 0.0)
            pool.memset(ckv[:], 0.0)
            pool.drain()
            pool.memset(X[NS:128, 2, :], 0.0)
            pool.drain()
            pool.memset(qsr, 0.0)
            pool.memset(ocn, 0.0)
            pool.memset(qsT, 0.0)
            pool.memset(vt[:, :, 512:576], 0.0).then_inc(S("zeroed"), 1)
            pool.wait_ge(S("zeroed"), 2)
            pool.drain()
            pool.drain()
            pool.memset(ckv[0:NS, 2, ONE:LAT], 1.0)
            pool.drain()
            pool.memset(ckv[:, 0:2, ONE:LAT], 1.0).then_inc(S("zeroed"), 1)
            pool.dma_start(wr[:], w_router[0].rearrange("(k p) e -> p k e", p=128)).then_inc(S("wr_in"), 16)
            pool.dma_start(br[:], b_router[0:1].partition_broadcast(128)).then_inc(S("wr_in"), 16)
            pool.dma_start(conv_s[0, :, 0:W - 1 - DEC_T, :], state_conv[0, :, DEC_T:W - 1, :]).then_inc(S("out"), 16)
            pool.wait_ge(S("x_T"), 6)
            pool.memset(glu[:, :, 0:W - 1], 0.0)
            pool.memset(glu[:, :, SEG0:GLU_W].rearrange("p c (s u) -> p c s u", u=SEG)[:, :, :, SEG - 1:SEG], 0.0)
            pool.memset(acc, 0.0).then_inc(S("conv_zero"), 1)
            pool.wait_ge(S("proj_done"), 3 + 2 * CC)
            pool.memset(ck[0][:, :, ONE:LAT], 1.0)
            pool.memset(ck[1][:, :, ONE:LAT], 1.0).then_inc(S("ck_ones"), 1)
            pool.wait_ge(S("ckv_done"), 3)
            pool.dma_start(lat_p[0, 0].rearrange("(c p) d -> p c d", p=128), ckv[:, 0:2, LAT:CROW]).then_inc(S("out"), 16)
            pool.dma_start(rope_p[0, 0].rearrange("(c p) d -> p c d", p=128), ckv[:, 0:2, 0:DR]).then_inc(S("out"), 16)
            pool.dma_start(lat_s[0].rearrange("b t d -> (b t) d"), ckv[0:NS, 2, LAT:CROW]).then_inc(S("out"), 16)
            pool.dma_start(rope_s[0].rearrange("b t d -> (b t) d"), ckv[0:NS, 2, 0:DR]).then_inc(S("out"), 16)
            pool.wait_ge(S("snew"), 1)
            v = snew[0:NS].rearrange("p (s h q) -> p s h q", s=8, h=8)
            pool.affine_select(out=v, in_=v, compare_op=ALU.is_ge, fill=-1e30, base=0,
                               pattern=[[-8, 8], [0, 8], [0, 8]], channel_multiplier=1).then_inc(S("snew_m"), 1)
            pool.wait_ge(S("snew_m"), 1)
            pool.affine_select(out=v, in_=v, compare_op=ALU.is_ge, fill=-1e30, base=0,
                               pattern=[[8, 8], [0, 8], [1, 8]], channel_multiplier=-1).then_inc(S("snew_m"), 1)
            def rope_squares(n, t, first):
                pool.wait_ge(S(f"ck_in{t}"), page_count(n, t))
                pool.wait_ge(S(f"ck2_in{t}"), page_count(n, t))
                if not first:
                    pool.wait_ge(S("rss_done"), n)
                pool.tensor_tensor(sqr[:], ck[t][:, :, 0:DR], ck[t][:, :, 0:DR], ALU.mult).then_inc(S("sqr"), 1)
            rope_squares(0, 0, True)
            pool.wait_ge(S("q_ss"), NC)
            pool.wait_ge(S("k_ss"), NC)
            pool.wait_ge(S("glu"), CC)

            def tap_products(c):
                pool.tensor_tensor(s_prod.rearrange("p (s q) j -> p s q j", s=DEC_B), windows(c),
                                   cw[:, 0:W * CC].rearrange("p (j c) -> p c j", c=CC)[:, bass.ds(c, 1), :].unsqueeze(1)
                                   .broadcast_to([128, DEC_B, DEC_T, W]), ALU.mult).then_inc(S("s_prod"), 1)
            tap_products(0)
            pool.wait_ge(S("rows_ev"), 1)
            for b in range(DEC_B):
                pool.dma_start(conv_s[0, b, W - 1 - DEC_T:W - 1, :], row_out[8 * b:8 * b + 8, :]).then_inc(S("out"), 16)
            pool.dma_start(conv_p[0, 0], row_out2[0:W - 1, :]).then_inc(S("out"), 16)
            with pool.Fori(0, 3) as i:
                rope_squares(2 * i + 1, 1, False)
                pool.wait_ge(S("s_sum"), i + 1)
                tap_products(i + 1)
                rope_squares(2 * i + 2, 0, False)
            rope_squares(7, 1, False)
            pool.wait_ge(S("ln_in"), 32)
            for c in range(NC):
                pool.wait_ge(S("ln"), c + 1)
                pool.tensor_tensor(conv_t[:, c, :], conv_t[:, c, :], lng, ALU.mult)
                pool.drain()
                pool.tensor_tensor(conv_t[:, c, :], conv_t[:, c, :], lnb, ALU.add).then_inc(S("ln_rows"), 1)
            for c in range(NC):
                pool.wait_ge(S("eg"), CC + c + 1)
                pool.tensor_tensor(conv_t[:, c, :], conv_t[:, c, :], ez[:, c, :], ALU.mult).then_inc(S("ln_rows"), 1)
            pool.wait_ge(S("attn_rows"), 1)
            pool.memset(bdn, 0.0)
            pool.memset(lgT[:], 0.0)
            pool.memset(zero_rows, 0.0)
            pool.memset(GT[:], 0.0).then_inc(S("moe_zero"), 1)
            pool.wait_ge(S("moe_zero"), 1)
            pool.dma_start(bdn[0:NE, :], b_down[0]).then_inc(S("bdn_in"), 16)
            pool.wait_ge(S("merged"), 6)
            pool.drain()
            pool.memset(xn2[NS:128, 2, :], 0.0)
            pool.drain()
            pool.memset(ysb, 0.0).then_inc(S("y_ev"), 2)
            pool.memset(selT, 0.0).then_inc(S("selT"), 1)
            pool.memset(bias, 0.0).then_inc(S("moe_zero"), 1)

        @block.tensor
        def _(pe):
            def mm(out, lhsT, rhs, a, b):
                return pe.matmul(out, lhsT, rhs, start=a, stop=b)

            def tr(out, in_, n=128):
                return pe.transpose(out, in_, ident[0:n, 0:n])

            pe.wait_ge(S("cst_in"), 16)
            pe.wait_ge(S("rows_in"), 16 * 7)
            tr(PS[7][:, 0:124], rows1[:], 124)
            tr(PS[7][:, 128:159], rows2[:], 31).then_inc(S("gains_T"), 1)
            for g in range(6):
                c, n = g // 2, CHUNKS[g // 2][1]
                pe.wait_ge(S("xn"), c + 1)
                for j in range(4):
                    k = 4 * (g % 2) + j
                    last = tr(PS[g][:, 128 * j:128 * j + n], xn[0:n, c, 128 * k:128 * k + 128], n)
                last.then_inc(S("x_T"), 1)
            pe.wait_ge(S("win_in"), 32)
            pe.wait_ge(S("xT"), 6)
            for c in ORDER:
                r, n = CHUNKS[c]
                for k in range(KD):
                    mm(PS[2 * c][0:n, 0:QL], xT[:, k, r:r + n], win[:, k, 1024:1408], k == 0, k == KD - 1)
                for k in range(KD):
                    last = mm(PS[2 * c + 1][0:n, 0:288], xT[:, k, r:r + n], win[:, k, 1408:1696], k == 0, k == KD - 1)
                last.then_inc(S("proj_done"), 1)
                if c == ORDER[0]:
                    pe.wait_ge(S("st_in"), 32)
                    pe.wait_ge(S("gains"), 1)
                    for cc in range(CC):
                        for i in range(2):
                            last = tr(PS[6 + cc // 2][:, 256 * (cc % 2) + 120 * i:256 * (cc % 2) + 120 * i + 120],
                                      st_rows[:, i, 128 * cc:128 * cc + 128], 120)
                    last.then_inc(S("state_T"), 1)

            def conv_in(c):
                a, g = (PS[6], PS[7]) if c % 2 == 0 else (PS[0], PS[1])
                if c == 0:
                    pe.wait_ge(S("state_ev"), CC)
                    pe.wait_ge(S("winc_in"), 32)
                if c == 1:
                    pe.wait_ge(S("ckv_done"), 2)
                if c >= 2:
                    pe.wait_ge(S("glu"), c - 1)
                for k in range(KD):
                    last = mm(g[:, 0:T], win[:, k, DC + 128 * c:DC + 128 * c + 128], xT[:, k, :], k == 0, k == KD - 1)
                last.then_inc(S("proj_done"), 1)
                for k in range(KD):
                    last = mm(a[:, 0:T], win[:, k, 128 * c:128 * c + 128], xT[:, k, :], k == 0, k == KD - 1)
                last.then_inc(S("proj_done"), 1)

            def q_up(i):
                r, n = CHUNKS[ORDER[i]]
                if i == 0:
                    pe.wait_ge(S("wuq_in"), 16)
                    pe.wait_ge(S("qlT"), 3)
                else:
                    pe.wait_ge(S("q_rope"), i)
                for hb in range(2):
                    for j in range(3):
                        last = mm(PS[4 + hb][0:n, 0:384], qlT[:, j, r:r + n], wuq[:, j, 384 * hb:384 * hb + 384], j == 0, j == 2)
                last.then_inc(S("q_up"), 1)

            def kv_up(i):
                r, n = CHUNKS[ORDER[i]]
                if i:
                    pe.wait_ge(S("glu"), 2 + i)
                for b, w in (((2, wk),), ((6, wk), (7, wv)), ((0, wk), (1, wv)))[i]:
                    for l in range(2):
                        last = mm(PS[b][0:n, 0:512], ckvT[:, l, r:r + n], w[:, l, :], l == 0, l == 1)
                last.then_inc(S("kv_up"), 1)

            conv_in(0)
            pe.wait_ge(S("ckv_done"), 3)
            pe.wait_ge(S("ql_done"), 3)
            for c, (r, n) in enumerate(CHUNKS):
                for l in range(2):
                    tr(PS[2 + c // 2][:, 256 * (c % 2) + 128 * l:256 * (c % 2) + 128 * l + n],
                       ckv[0:n, c, LAT + 128 * l:LAT + 128 * l + 128], n)
            tr(PS[3][:, 256:256 + NS], ckv[0:NS, 2, 0:128], NS)
            for c in ORDER:
                n = CHUNKS[c][1]
                for j in range(3):
                    dst = PS[3][:, 320 + NS * j:320 + NS * j + NS] if c == 2 else PS[4 + c][:, 128 * j:128 * j + n]
                    last = tr(dst, ql[0:n, c, 128 * j:128 * j + 128], n)
                last.then_inc(S("ql_T"), 1)
            conv_in(1)
            q_up(0)
            pe.wait_ge(S("wkv_in"), 64)
            pe.wait_ge(S("latT"), 3)
            for hp in range(4):
                for l in range(2):
                    last = tr(PS[2 + hp // 2][:, 256 * (hp % 2) + 128 * l:256 * (hp % 2) + 128 * l + 128],
                              wk[:, l, 128 * hp:128 * hp + 128])
            last.then_inc(S("wk_T"), 1)
            conv_in(2)
            pe.wait_ge(S("wkT"), 2)
            kv_up(0)
            q_up(1)
            conv_in(3)
            pe.wait_ge(S("q_done"), 1)
            pe.wait_ge(S("k_sq"), 1)
            for hp in range(4):
                tr(PS[3][:, 64 * hp:64 * hp + 64], qsn[0:NS, 128 * hp:128 * hp + 128], NS)
            for h in range(H):
                last = tr(PS[2][:, 64 * h:64 * h + 64], qsr[0:NS, 32 * h:32 * h + 128], NS)
            last.then_inc(S("qs_T"), 1)
            kv_up(1)
            pe.wait_ge(S("qsT"), 1)
            for l in range(2):
                for hp in range(4):
                    last = mm(PS[2 + l][:, 128 * hp:128 * hp + 128], wkT[:, hp, 128 * l:128 * l + 128], qsT[:, hp, :], True, True)
            last.then_inc(S("q_abs"), 1)
            q_up(2)
            pe.wait_ge(S("qabs"), 2)
            for l in range(2):
                mm(PS[2][0:NS, :], ckvT[:, l, SEQ:T], qabs[:, l, :], l == 0, False)
            mm(PS[2][0:NS, :], krn[:], qrT[:], False, True).then_inc(S("s_new"), 1)
            kv_up(2)
            for i in range(4):
                c, src = ((0, kt), (0, qt), (1, kt), (1, qt))[i]
                pe.wait_ge(S("k_done"), 2 + c)
                pe.wait_ge(S("q_done"), 2 + c)
                if i == 0:
                    pe.wait_ge(S("snew"), 1)
                    pe.wait_ge(S("v_done"), 1)
                for hb in range(2):
                    b = 2 * i + hb
                    if i >= 2:
                        pe.wait_ge(S("heads_ev"), b - 3)
                    for h in range(4):
                        last = tr(PS[(2, 3, 6, 7)[b % 4]][0:DQ, 128 * h:128 * h + 128],
                                  src[c][:, DQ * (4 * hb + h):DQ * (4 * hb + h) + DQ])
                    last.then_inc(S("heads_T"), 1)
            pe.wait_ge(S("v_done"), 2)
            for c in range(CC):
                tr(PS[1][0:W - 1, 128 * c:128 * c + 128], glu[:, c, SEQ:SEQ + W - 1])
            for c in range(CC):
                last = tr(PS[0][0:NS, 128 * c:128 * c + 128], gpk[:, c, :])
            last.then_inc(S("rows_T"), 1)

            pe.wait_ge(S("heads_ev"), 8)
            pe.wait_ge(S("rows_ev"), 1)
            pe.wait_ge(S("snew"), 1)

            def part_max(n):
                pe.wait_ge(S("m_part"), n + 1)
                tr(PS[6][:, 0:128], m1[:]).then_inc(S("m_T"), 1)

            def part_spread(n):
                pe.wait_ge(S("m_diag"), n + 1)
                mm(PS[6][:, 128:256], ones, dg[:], True, True).then_inc(S("m_all"), 1)

            def part_out(n, t):
                pe.wait_ge(S("probs"), n + 1)
                for b in range(PAGES):
                    mm(PS[7][0:64, 0:260], s_all[t][:, b, :], ck[t][:, b, ONE:CROW], b == 0, False)
                mm(PS[7][0:64, 0:260], pn[:], ckv[:, 2, ONE:CROW], False, True).then_inc(S("ck_used"), 1)

            def part_outT(n):
                pe.wait_ge(S("oc_n"), n + 1)
                for l in range(2):
                    last = tr(PS[6][:, 256 + 128 * l:384 + 128 * l], ocn[:, 128 * l:128 * l + 128])
                last.then_inc(S("oc_T"), 1)

            def sequence(n, t, first):
                pair = n - t
                def transposes(b):
                    m = n * PAGES + b
                    if b == PAGES // 2:
                        pe.wait_ge(S(f"ck2_in{t}"), page_count(n, t))
                    if not (first and b < 2):
                        pe.wait_ge(S("cT"), m - 1)
                    tr(PS[b % 2][:, 0:128], ck[t][:, b, LAT:LAT + 128])
                    tr(PS[b % 2][:, 128:256], ck[t][:, b, LAT + 128:CROW])
                    tr(PS[b % 2][:, 256:384], ck[t][:, b, 0:128]).then_inc(S("c_T"), 1)
                pe.wait_ge(S(f"ck_in{t}"), page_count(n, t))
                if first:
                    pe.wait_ge(S("ck_ones"), 1)
                transposes(0)
                for b in range(PAGES):
                    m = n * PAGES + b
                    if b < PAGES - 1:
                        transposes(b + 1)
                    pe.wait_ge(S("cT"), m + 1)
                    if not (first and b < 2):
                        pe.wait_ge(S("sq"), m - 1)
                    for l in range(2):
                        last = mm(PS[2 + b % 2][:, :], cT[:, b % 2, 128 * l:128 * l + 128], wk[:, l, :], l == 0, l == 1)
                    last.then_inc(S("keys"), 1)
                    half = PS[4 + b // 4][:, 128 * (b % 4):128 * (b % 4) + 128]
                    if b % 4 == 0 and not first:
                        pe.wait_ge(S("s_half"), 2 * n + b // 4 - 1)
                    cols = bass.ds(pair * 64, 128)
                    for l in range(2):
                        mm(half, cT[:, b % 2, 128 * l:128 * l + 128], qabs[:, l, cols], l == 0, False)
                    mm(half, cT[:, b % 2, 256:384], qrT[:, cols], False, True).then_inc(S("scores"), 1)
                    if not first:
                        if b == 1:
                            part_max(n - 1)
                        if b == 2:
                            part_spread(n - 1)
                        if b == 4:
                            part_out(n - 1, 1 - t)
                        if b == 6:
                            part_outT(n - 1)
            sequence(0, 0, True)
            with pe.Fori(0, 3) as i:
                sequence(2 * i + 1, 1, False)
                sequence(2 * i + 2, 0, False)
            sequence(7, 1, False)
            part_max(7)
            part_spread(7)
            part_out(7, 1)
            part_outT(7)

            def p_scores(h):
                if h >= 2:
                    pe.wait_ge(S("p_exp"), h - 1)
                mm(PS[h % 2][:, 0:384], ident, causal3, True, False)
                mm(PS[h % 2][:, 0:128], qT[0:DQ, h, 0:128], kT[0:DQ, h, 0:128], False, False)
                mm(PS[h % 2][:, 128:384], qT[0:DQ, h, 128:256], kT[0:DQ, h, :], False, True).then_inc(S("p_sc"), 1)

            def p_trans(h):
                pe.wait_ge(S("p_exp"), h + 1)
                if h >= 2:
                    pe.wait_ge(S("p_T"), h - 1)
                for j in range(3):
                    last = tr(PS[2 + h % 2][:, 128 * j:128 * j + 128], pr[h % 2][:, j, :])
                last.then_inc(S("p_tr"), 1)

            def p_out(h):
                pe.wait_ge(S("p_T"), h + 1)
                if h >= 2:
                    pe.wait_ge(S("p_o"), h - 1)
                if h == 1:
                    pe.wait_ge(S("ln"), 3)
                v = slice(DV * h, DV * h + 128)
                mm(PS[4 + h % 2][:, 0:128], pT[h % 2][:, 0, :], vt[:, 0, v], True, True)
                mm(PS[4 + h % 2][:, 128:256], pT[h % 2][:, 1, :], vt[:, 0, v], True, False)
                mm(PS[4 + h % 2][:, 128:256], pT[h % 2][:, 2, :], vt[:, 1, v], False, True).then_inc(S("p_out"), 1)
            pe.wait_ge(S("s_half"), 2 * DEC_B)
            pe.wait_ge(S("sq"), PAGES * DEC_B)
            pe.wait_ge(S("conv_done"), 1)
            pe.wait_ge(S("ocT"), DEC_B)
            for c in range(NC):
                for j in range(CC):
                    last = tr(PS[(6, 7, 5)[c]][:, 128 * j:128 * j + 128], acc[:, j, 128 * c:128 * c + 128])
                last.then_inc(S("conv_T"), 1)

            def mix_T(src, ready, c, bank):
                n = CHUNKS[c][1]
                pe.wait_ge(S(ready), c + 1)
                for j in range(CC):
                    last = tr(bank[:, 128 * j:128 * j + n], src[0:n, c, 128 * j:128 * j + 128], n)
                last.then_inc(S("mix_T"), 1)
            for h in range(H + 2):
                if h < H:
                    p_scores(h)
                if 1 <= h <= H:
                    p_trans(h - 1)
                if h >= 2:
                    p_out(h - 2)
                if h == 2:
                    pe.wait_ge(S("ln"), 2)
                    for hh in range(H):
                        for l in range(2):
                            last = mm(PS[7][0:NS, DV * hh:DV * hh + DV], ocT[:, l, 64 * hh:64 * hh + 64],
                                      wv[:, l, DV * hh:DV * hh + DV], l == 0, l == 1)
                    last.then_inc(S("attn_s"), 1)
            pe.wait_ge(S("attn_rows"), 1)
            for c in range(NC):
                if c == 2:
                    pe.wait_ge(S("mixT"), 1)
                mix_T(conv_t, "conv_n", c, PS[(6, 7, 6)[c]])
            pe.wait_ge(S("wout_in"), 16)
            pe.wait_ge(S("p_exp"), H)
            pe.wait_ge(S("p_T"), H)
            pe.wait_ge(S("p_o"), H)

            def merge(c, hf, ks):
                r, n = CHUNKS[c]
                for k in ks:
                    last = mm(PS[(4, 0, 2)[c] + hf][0:n, :], xT[:, k, r:r + n], wout[:, k, 512 * hf:512 * hf + 512],
                              k == 0, k == KD - 1)
                return last
            for c in range(NC):
                pe.wait_ge(S("mixT"), c + 1)
                for hf in range(2):
                    merge(c, hf, range(4))
            for c in range(NC):
                if c == 2:
                    pe.wait_ge(S("mixT"), 4)
                mix_T(attn_t, "attn_n", c, PS[(7, 6, 7)[c]])
            pe.wait_ge(S("mixT"), 6)

            def h_T(i):
                c, n = ORDER[i], CHUNKS[ORDER[i]][1]
                pe.wait_ge(S("xn2"), i + 1)
                if i == 2:
                    pe.wait_ge(S("hT"), 2)
                for g in range(2):
                    for j in range(4):
                        k = 4 * g + j
                        last = tr(PS[(6, 4, 6)[i] + g][:, 128 * j:128 * j + n], xn2[0:n, c, 128 * k:128 * k + 128], n)
                    last.then_inc(S("h_T"), 1)

            def logits(i):
                r, n = CHUNKS[ORDER[i]]
                pe.wait_ge(S("hT"), 2 * i + 2)
                for k in range(KD):
                    last = mm(PS[2][0:NE, r:r + n], wr[:, k, :], xT[:, k, r:r + n], k == 0, k == KD - 1)
                return last
            for i, c in enumerate(ORDER):
                for hf in range(2):
                    merge(c, hf, range(4, 8)).then_inc(S("merged"), 1)
                if i == 1:
                    h_T(0)
            pe.wait_ge(S("wr_in"), 32)
            h_T(1)
            logits(0)
            h_T(2)
            logits(1)
            logits(2).then_inc(S("route_mm"), 1)
            pe.wait_ge(S("lgT"), 1)
            for c in range(NC):
                last = tr(PS[3][:, 32 * c:32 * c + 32], lgT[:, 128 * c:128 * c + 128], 32)
            last.then_inc(S("route_mm"), 1)
            pe.wait_ge(S("routed"), 1)
            for c in range(NC):
                last = mm(PS[1][0:NE, 0:128], M[:, c, :], ones, c == 0, c == NC - 1)
            last.then_inc(S("route_mm"), 1)
            mm(PS[0][:, 0:NC * NE], upper, M.rearrange("p c e -> p (c e)"), True, False)
            mm(PS[0][:, NE:3 * NE], ones, M[:, 0:2, :].rearrange("p c e -> p (c e)"), False, False)
            mm(PS[0][:, 2 * NE:3 * NE], ones, M[:, 0, :], False, True).then_inc(S("route_mm"), 1)
            pe.wait_ge(S("routed"), 2)
            mm(PS[4][0:NE, 0:128], ones[:, 0:NE], extra_all, True, True).then_inc(S("route_mm"), 1)
            pe.wait_ge(S("routed"), 3)
            for c in range(NC):
                tr(PS[5][0:NE, 128 * c:128 * c + 128], lg[:, c, :])
                last = tr(PS[6][0:NE, 128 * c:128 * c + 128], G[:, c, :])
            last.then_inc(S("route_mm"), 1)
            pe.wait_ge(S("routed"), 4)
            mm(PS[2][0:NE, 0:128], upper[:, 0:NE], extra_all, True, True)
            mm(PS[4][0:1, 128:256], extra_all[:, 0:1], upper, True, True)
            mm(PS[4][0:1, 256:384], ones[:, 0:1], extra_all, True, True).then_inc(S("route_mm"), 1)

            def y_bias(q):
                c, hf = q // 2, q % 2
                mm(PS[(0, 1, 2, 4, 0, 1)[q]][:, :], GT[:, 128 * c:128 * c + 128], bdn[:, 512 * hf:512 * hf + 512], True, True)\
                    .then_inc(S("y_bias"), 1)
            pe.wait_ge(S("routed"), 5)
            pe.wait_ge(S("bdn_in"), 16)
            y_bias(0)
            y_bias(1)
            pe.wait_ge(S("routed"), 6)
            mm(PS[6][0:1, 384:512], ones[:, 0:1], wide[2], True, True)
            for c in range(NC):
                cs = slice(128 * c, 128 * c + 128)
                mm(PS[7][:, cs], posT_all[:, cs], wide[0], True, False)
                mm(PS[7][:, cs], ones, wide[1], False, True)
                last = mm(PS[3][:, cs], GT[:, cs], wide[0], True, True)
            last.then_inc(S("route_mm"), 1)

            def gather(v):
                pe.wait_ge(S("sel"), v)
                for k in range(KD):
                    for c in range(NC):
                        last = mm(PS[5 + k // 4][:, 128 * (k % 4):128 * (k % 4) + 128],
                                  xn2[:, c, 128 * k:128 * k + 128], sel[:, c, :], c == 0, c == NC - 1)
                last.then_inc(S("gathered"), 1)

            def item(i, t):
                e = pe.value_load(tab[0:1, bass.ds(2 * i + (t + TAB_E), 1)], min_val=0, max_val=NE - 1)
                return e, pe.value_load(odd_tab[0:1, bass.ds(e, 1)], min_val=0, max_val=1)

            def gate_up(i, t, e, odd):
                n = 2 * i + t
                if t == 0:
                    pe.wait_ge(S("xg"), i + 1)
                pe.wait_ge(S("bias_in"), 16 * e + 16)
                pe.wait_ge(S("gu_ev"), n + 1)
                if t == 1:
                    pe.wait_ge(S("y_add"), 6 * i + 5)
                xs = [xg[:, k, 64 * t:64 * t + 64] for k in range(KD)]
                for q in range(4):
                    last = mm(PS[q // 2][64 * (q % 2):64 * (q % 2) + 64, :], one_row,
                              bias[:, 512 * q:512 * q + 512], True, False)
                last.then_inc(S("bias_used"), 1)

                def rows(k, part):
                    if k % 2 == 0 and part == 0:
                        pe.wait_ge(S(f"gu_in{k // 2}"), 8 * e + 16)
                    elif k % 2 == 0 and part == 3:
                        pe.wait_ge(S(f"gu_odd{k // 2}"), 8 * e + 8)
                    elif k % 2 == 0:
                        pe.wait_ge(S(f"gu_in{k // 2}"), 16 * e + 16)
                    for q in range(4):
                        at = parts[part] + 2048 * (k % 4) + 512 * q
                        last = mm(PS[q // 2][64 * (q % 2):64 * (q % 2) + 64, :], xs[k], sb[:, at:at + 512], False, k == KD - 1)
                    if k == KD - 1:
                        last.then_inc(S("gu_done"), 1)
                    elif k % 2 == 1:
                        last.then_inc(S(f"gu_used{k // 2}"), 1)
                with pe.If(odd < 1):
                    for k in range(4):
                        rows(k, 0)
                with pe.If(odd > 0):
                    for k in range(4):
                        rows(k, 3)
                for k in range(4, KD):
                    rows(k, 1)

            def combine(v, last_pair=False):
                pe.wait_ge(S("selT"), v + 1)
                pe.wait_ge(S("y_ev"), 2 * v + 2)
                for c in range(NC):
                    for hf in range(2):
                        q = 2 * c + hf
                        if q == 3 and not last_pair:
                            pe.wait_ge(S("gu_ev"), 2 * v + 2)
                        if q == 5:
                            pe.wait_ge(S("y_add"), 6 * v + 1)
                        mm(PS[(5, 6, 7, 1, 0, 5)[q]][:, :], selT[:, hf, 128 * c:128 * c + 128], ysb[:, hf, :], True, True)\
                            .then_inc(S("combined"), 1)

            def down(i, t, e):
                n = 2 * i + t
                pe.wait_ge(S("h"), n + 1)
                for c in range(4):
                    last = tr(PS[4][:, 128 * c:128 * c + 128], hsb[:, 128 * c:128 * c + 128])
                last.then_inc(S("h_tr"), 1)
                for k in range(KD):
                    if k in (0, 2):
                        pe.wait_ge(S("h_ev"), 2 * n + 1 + k // 2)
                    if k % 4 == 0:
                        pe.wait_ge(S(f"dn_in{k // 4}"), 16 * e + 16)
                    lhsT = hT[:, 128 * (k % 4) + 64 * (k // 4):128 * (k % 4) + 64 * (k // 4) + 64]
                    for hf in range(2):
                        p = 64 * (t ^ hf)
                        last = mm(PS[2 + hf][p:p + 64, :], lhsT, dn_w[:, k, 512 * hf:512 * hf + 512], k == 0, k == KD - 1)
                    if k == 3:
                        last.then_inc(S("dn_used0"), 1)
                last.then_inc(S("dn_done"), 1)

            gsb_, usb_, sgb_, hsb, hT = gsb
            pe.wait_ge(S("moe_zero"), 2)
            pe.wait_ge(S("odd_in"), 16)
            pe.wait_ge(S("table"), 1)
            gather(1)
            y_bias(2)
            y_bias(3)
            for q in (4, 5):
                pe.wait_ge(S("ybias"), q - 3)
                y_bias(q)
            pe.wait_ge(S("ybias"), 6)
            n_iter = pe.value_load(tab[0:1, 0:1], min_val=NE // 2, max_val=MAX_ITER)
            with pe.Fori(0, n_iter) as i:
                e0, odd0 = item(i, 0)
                gate_up(i, 0, e0, odd0)
                combine(i)
                down(i, 0, e0)
                e1, odd1 = item(i, 1)
                gate_up(i, 1, e1, odd1)
                pe.wait_ge(S("selg"), i + 1)
                pe.wait_ge(S("h_ev"), 4 * i + 2)
                pe.wait_ge(S("y_add"), 6 * i + 6)
                for c in range(NC):
                    tr(PS[4][:, 128 * c:128 * c + 128], selg[:, c, 0:128])
                    last = tr(PS[7][:, 128 * c:128 * c + 128], selg[:, c, 64:192])
                last.then_inc(S("sel_T"), 1)
                gather(i + 2)
                pe.wait_ge(S("selT"), i + 2)
                down(i, 1, e1)
            pe.wait_ge(S("xg"), n_iter + 1)
            combine(n_iter, True)

        @block.scalar
        def _(act):
            act.dma_start(cst[:], c_pack).then_inc(S("cst_in"), 16)
            act.dma_start(rows2[0:8, :], norm_mix[0].rearrange("(k p) -> k p", p=128)).then_inc(S("rows_in"), 16)
            act.dma_start(rows2[8:11, :], norm_q_lat[0].rearrange("(k p) -> k p", p=128)).then_inc(S("rows_in"), 16)
            act.dma_start(rows2[11:15, :], conv_b[0].rearrange("(k p) -> k p", p=128)).then_inc(S("rows_in"), 16)
            act.dma_start(rows2[15:19, :], norm_out_conv[0].rearrange("(k p) -> k p", p=128)).then_inc(S("rows_in"), 16)
            act.dma_start(rows2[19:23, :], norm_out_attn[0].rearrange("(k p) -> k p", p=128)).then_inc(S("rows_in"), 16)
            act.dma_start(rows2[23:31, :], norm_ffn[0].rearrange("(k p) -> k p", p=128)).then_inc(S("rows_in"), 16)
            act.dma_start(rows1[:], conv_w[0].rearrange("t (c p) -> (t c) p", p=128)).then_inc(S("rows_in"), 16)
            act.dma_start(cos[:], c_cos).then_inc(S("rope_in"), 16)
            act.dma_start(sin[:], c_sin).then_inc(S("rope_in"), 16)
            act.preload_act_table_set("natural_log_exp_and_others")

            def copy(out, in_):
                return act.activation(out, in_, ACT.Copy)

            def root(out, in_, scale, own_input=True):
                p, tmp = in_.shape[0], lnx
                k = 1
                for d in in_.shape[1:]:
                    k *= d
                tmp = lnx[0:p, 0:k]
                if len(in_.shape) == 3:
                    tmp = tmp.rearrange("p (a b) -> p a b", a=in_.shape[1])
                if own_input:
                    act.drain()
                act.activation(tmp, in_, ACT.Ln, bias=eps[0:p, :], scale=scale)
                act.drain()
                return act.activation(out, tmp, ACT.Exp, scale=-0.5)

            def sigmoid_of(out, in_):
                act.activation(out, in_, ACT.Exp, scale=-1.0)
                act.drain()
                act.activation(out, out, ACT.Ln, bias=ones[:, 0:1])
                act.drain()
                return act.activation(out, out, ACT.Exp, scale=-1.0)

            sq_x = view(R_GU + NC * QL + 2 * T + 3 * T + 2 * T, D)
            act.wait_ge(S("cst_in"), 16)
            act.wait_ge(S("x_in"), 32)
            act.wait_ge(S("zeroed"), 1)
            for c, (r, n) in enumerate(CHUNKS):
                act.drain()
                act.activation(sq_x[0:n], X[0:n, c, :], ACT.Square, accum_out=ss[0:n, c:c + 1])
            root(rs[:, 0:3], ss[:, 0:3], 1 / D).then_inc(S("root"), 1)
            for i, c in enumerate(ORDER):
                n = CHUNKS[c][1]
                act.wait_ge(S("proj_done"), i + 1)
                act.activation(sq_x[0:n, 0:QL], PS[2 * c][0:n, 0:QL], ACT.Square, accum_out=ss[0:n, 4 + 2 * c:5 + 2 * c])
                act.activation(sq_x[0:n, 512:768], PS[2 * c + 1][0:n, 0:KVL], ACT.Square, accum_out=ss[0:n, 5 + 2 * c:6 + 2 * c])
                act.drain()
                act.activation(lnx[0:n, 0:1], ss[0:n, 4 + 2 * c:5 + 2 * c], ACT.Ln, bias=eps[0:n, :], scale=1 / QL)
                act.activation(lnx[0:n, 1:2], ss[0:n, 5 + 2 * c:6 + 2 * c], ACT.Ln, bias=eps[0:n, :], scale=1 / KVL)
                act.drain()
                act.activation(rs[0:n, 4 + 2 * c:6 + 2 * c], lnx[0:n, 0:2], ACT.Exp, scale=-0.5).then_inc(S("rl"), 1)

            def gate_exp(c):
                act.wait_ge(S("proj_done"), 3 + 2 * c + 1)
                if c >= 2:
                    act.wait_ge(S("glu"), c - 1)
                sigmoid_of(eg[:, c % 2, :], PS[7 if c % 2 == 0 else 1][:, 0:T]).then_inc(S("eg"), 1)

            def q_copy(i):
                c = ORDER[i]
                n = CHUNKS[c][1]
                act.wait_ge(S("q_up"), i + 1)
                q = qt[c][0:n].rearrange("p (h d) -> p h d", h=H)
                for hb in range(2):
                    src = PS[4 + hb][0:n, 0:384].rearrange("p (h d) -> p h d", h=4)
                    copy(q[:, 4 * hb:4 * hb + 4, 0:DN], src[:, :, 0:DN]).then_inc(S("q_nope"), 1)

            def q_root(i):
                c = ORDER[i]
                n = CHUNKS[c][1]
                act.wait_ge(S("q_rope"), i + 1)
                act.activation(sqs[0:n, 0, :], qt[c][0:n], ACT.Square).then_inc(S("q_sq"), 1)
                act.wait_ge(S("q_ss"), i + 1)
                root(r8[0:n, 0, :], s8[0:n, 0, :], 1 / DQ).then_inc(S("q_r"), 1)

            def k_root(i):
                c = ORDER[i]
                n = CHUNKS[c][1]
                act.wait_ge(S("kv_up"), i + 1)
                act.activation(sqs[0:n, 1, 0:512], PS[(2, 6, 0)[i]][0:n, :], ACT.Square).then_inc(S("k_sq"), 1)
                if i:
                    copy(vt[:, c, 0:512], PS[(7, 1)[i - 1]][:, :]).then_inc(S("v_done"), 1)
                act.wait_ge(S("k_ss"), i + 1)
                root(r8[0:n, 1 if i else 2, :], s8[0:n, 1, :], 1 / DQ).then_inc(S("k_r"), 1)

            gate_exp(0)
            gate_exp(1)
            q_copy(0)
            act.wait_ge(S("wk_T"), 1)
            for j in range(2):
                copy(wkT[:, 2 * j:2 * j + 2, :], PS[2 + j][:, :].rearrange("p (a b) -> p a b", a=2)).then_inc(S("wkT"), 1)
            q_root(0)
            gate_exp(2)
            k_root(0)
            q_copy(1)
            q_root(1)
            gate_exp(3)
            k_root(1)
            q_copy(2)
            q_root(2)
            k_root(2)
            act.wait_ge(S("rows_T"), 1)
            copy(row_out[:], PS[0][0:NS, :])
            copy(row_out2[0:W - 1, :], PS[1][0:W - 1, :])
            act.drain()
            act.nop().then_inc(S("rows_ev"), 1)

            def rk(n, half):
                act.wait_ge(S("ss_half"), 2 * n + half + 1)
                root(r8[:, 4 * half:4 * half + 4, :], s8[:, 4 * half:4 * half + 4, :], 1 / DQ, False).then_inc(S("rk"), 1)

            def probs(n, t):
                act.wait_ge(S("s_sub"), n + 1)
                act.activation(s_all[t], s_all[t], ACT.Exp, scale=SCALE)
                act.activation(pn[0:NS, :], pn[0:NS, :], ACT.Exp, scale=SCALE).then_inc(S("probs"), 1)

            def sequence(n, t, first):
                def take_T(b):
                    m = n * PAGES + b
                    act.wait_ge(S("c_T"), m + 1)
                    if not (first and b < 2):
                        act.wait_ge(S("scores"), m - 1)
                    copy(cT[:, b % 2, :], PS[b % 2][:, 0:384]).then_inc(S("cT"), 1)
                take_T(0)
                for b in range(PAGES):
                    m = n * PAGES + b
                    if b < PAGES - 1:
                        take_T(b + 1)
                    act.wait_ge(S("keys"), m + 1)
                    if not (first and b < 2):
                        act.wait_ge(S("kss"), m - 1)
                    act.activation(sqk[b % 2], PS[2 + b % 2][:, :], ACT.Square).then_inc(S("sq"), 1)
                    if b == 0 and not first:
                        rk(n - 1, 1)
                    if b == 3 and not first:
                        probs(n - 1, 1 - t)
                    if b == 4:
                        rk(n, 0)
            sequence(0, 0, True)
            with act.Fori(0, 3) as i:
                sequence(2 * i + 1, 1, False)
                sequence(2 * i + 2, 0, False)
            sequence(7, 1, False)
            rk(7, 1)
            probs(7, 1)

            def p_exp(h):
                act.wait_ge(S("p_m"), h + 1)
                if h >= 2:
                    act.wait_ge(S("p_o"), h - 1)
                    act.wait_ge(S("p_tr"), h - 1)
                act.activation(pr[h % 2][:, 0, :], PS[h % 2][:, 0:128], ACT.Exp, bias=pm[:, h % 2, 0:1], scale=SCALE,
                               accum_out=psm[:, h % 2, 0:1])
                act.activation(pr[h % 2][:, 1:3, :], PS[h % 2][:, 128:384].rearrange("p (a b) -> p a b", a=2), ACT.Exp,
                               bias=pm[:, h % 2, 1:2], scale=SCALE, accum_out=psm[:, h % 2, 1:2])
                act.drain()
                act.nop().then_inc(S("p_exp"), 1)

            def p_T(h):
                act.wait_ge(S("p_tr"), h + 1)
                if h >= 2:
                    act.wait_ge(S("p_out"), h - 1)
                copy(pT[h % 2], PS[2 + h % 2][:, 0:384].rearrange("p (a b) -> p a b", a=3)).then_inc(S("p_T"), 1)

            def row_squares(src, c, n, at):
                act.activation(scr[0:n, DC * c:DC * c + DC], src[0:n, c, :], ACT.Square, accum_out=ss[0:n, at + c:at + c + 1])
            act.wait_ge(S("mv"), 1)
            root(rs[:, 3:6], mv[:, :, 1], 1.0).then_inc(S("root"), 1)
            for h in range(H + 1):
                if h < H:
                    p_exp(h)
                if h >= 1:
                    p_T(h - 1)
                if h in (4, 5, 6):
                    act.wait_ge(S("ln_rows"), h - 3)
                    sigmoid_of(ez[:, h - 4, :], conv_t[:, h - 4, :]).then_inc(S("eg"), 1)
                if h == 8:
                    for c in range(NC):
                        act.wait_ge(S("ln_rows"), NC + c + 1)
                        row_squares(conv_t, c, 128, 6)
                    root(rs[:, 6:9], ss[:, 6:9], 1 / DC).then_inc(S("root"), 1)
            act.wait_ge(S("attn_rows"), 1)
            act.wait_ge(S("p_o"), H)
            for c, (r, n) in enumerate(CHUNKS):
                row_squares(attn_t, c, n, 0)
            root(rs[:, 0:3], ss[:, 0:3], 1 / DC).then_inc(S("root"), 1)
            for i, c in enumerate(ORDER):
                n = CHUNKS[c][1]
                act.wait_ge(S("h_rows"), i + 1)
                act.drain()
                act.activation(scr[0:n, 0:D], X[0:n, c, :], ACT.Square, accum_out=ss[0:n, 9 + c:10 + c])
                root(rs[0:n, 9 + c:10 + c], ss[0:n, 9 + c:10 + c], 1 / D).then_inc(S("root"), 1)
            act.wait_ge(S("gate_d"), 1)
            act.activation(gate4[:], gate4[:], ACT.Exp).then_inc(S("root"), 1)

            gsb_, usb_, sgb_, hsb, hT = gsb
            act.preload_act_table(ACT.Sigmoid)

            def sigmoid(i, t):
                act.wait_ge(S("g_min"), 2 * i + t + 1)
                act.activation(sgb_, gsb_, ACT.Sigmoid, scale=ALPHA).then_inc(S("sig"), 1)

            def h_rows_T(i, t):
                act.wait_ge(S("h_tr"), 2 * i + t + 1)
                for hf in range(2):
                    copy(hT[:, 256 * hf:256 * hf + 256], PS[4][:, 256 * hf:256 * hf + 256]).then_inc(S("h_ev"), 1)

            def y_rows(i, t):
                act.wait_ge(S("dn_done"), 2 * i + t + 1)
                if t == 0:
                    act.wait_ge(S("combined"), 6 * i + 6)
                copy(ysb[64 * t:64 * t + 64, 0, :], PS[2][64 * t:64 * t + 64, :])
                u = 64 * (1 - t)
                copy(ysb[u:u + 64, 1, :], PS[3][u:u + 64, :]).then_inc(S("y_ev"), 1)

            act.wait_ge(S("table"), 1)
            n_iter = act.value_load(tab[0:1, 0:1], min_val=NE // 2, max_val=MAX_ITER)
            with act.Fori(0, n_iter) as i:
                sigmoid(i, 0)
                h_rows_T(i, 0)
                y_rows(i, 0)
                sigmoid(i, 1)
                act.wait_ge(S("sel_T"), i + 1)
                copy(selT[:, 0, :], PS[4][:, 0:384])
                copy(selT[:, 1, :], PS[7][:, 0:384]).then_inc(S("selT"), 1)
                h_rows_T(i, 1)
                y_rows(i, 1)

        @block.vector
        def _(dve):
            def tt(out, a, b, op):
                return dve.tensor_tensor(out, a, b, op)

            def ts(out, a, s1, s2=None, op0=ALU.mult, op1=ALU.mult):
                return dve.tensor_scalar(out, a, s1, s2, op0, op1) if s2 is not None else dve.tensor_scalar(out, a, s1, None, op0)

            dve.wait_ge(S("gains_T"), 1)
            dve.wait_ge(S("zeroed"), 1)
            dve.tensor_copy(cw[:, 0:124], PS[7][:, 0:124])
            dve.tensor_copy(gc[:], PS[7][:, 128:159]).then_inc(S("gains"), 1)
            dve.wait_ge(S("root"), 1)
            for c, (r, n) in enumerate(CHUNKS):
                ts(xn[0:n, c, :], X[0:n, c, :], rs[0:n, c:c + 1]).then_inc(S("xn"), 1)
            dve.wait_ge(S("gains"), 1)
            for g in range(6):
                c, (r, n) = g // 2, CHUNKS[g // 2]
                k = 4 * (g % 2)
                dve.wait_ge(S("x_T"), g + 1)
                tt(xT[:, k:k + 4, r:r + n], PS[g][:, :].rearrange("p (a b) -> p a b", a=4)[:, :, 0:n],
                   bc(g_mix[:, k:k + 4], [128, 4, n], 2), ALU.mult).then_inc(S("xT"), 1)
            def seg(c, a, b):
                return glu[:, c, SEG0:GLU_W].rearrange("p (s u) -> p s u", u=SEG)[:, :, a:b]
            dve.wait_ge(S("g_in"), 80)
            tt(gqk[:], gqk[:], gkk[:], ALU.mult)
            dve.wait_ge(S("conv_zero"), 1)
            for c in range(CC):
                ts(acc[:, c, 0:SEQ], acc[:, c, 0:SEQ], g_cb[:, c:c + 1], None, ALU.add)

            def rotate(out1, out2, v, cs, sn, shape, tmp):
                k = 1
                for d in shape[1:]:
                    k *= d
                n = shape[0]
                ta, tb = rope_a[0:n, tmp:tmp + k], rope_b[0:n, tmp:tmp + k]
                if len(shape) == 4:
                    ta, tb = (z.rearrange("p (a b c) -> p a b c", a=shape[1], b=2) for z in (ta, tb))
                else:
                    ta, tb = (z.rearrange("p (b c) -> p b c", b=2) for z in (ta, tb))
                tt(ta, v, cs, ALU.mult)
                tt(tb, v, sn, ALU.mult)
                dve.drain()
                if len(shape) == 4:
                    a1, a2, b1, b2 = ta[:, :, 0, :], ta[:, :, 1, :], tb[:, :, 0, :], tb[:, :, 1, :]
                else:
                    a1, a2, b1, b2 = ta[:, 0, :], ta[:, 1, :], tb[:, 0, :], tb[:, 1, :]
                tt(out1, a1, b2, ALU.subtract)
                return tt(out2, a2, b1, ALU.add)

            dve.wait_ge(S("rope_in"), 32)
            dve.wait_ge(S("zeroed"), 3)
            for i, c in enumerate(ORDER):
                n = CHUNKS[c][1]
                dve.wait_ge(S("rl"), i + 1)
                ts(ql[0:n, c, :], PS[2 * c][0:n, 0:QL], rs[0:n, 4 + 2 * c:5 + 2 * c]).then_inc(S("ql_done"), 1)
                kv = PS[2 * c + 1]
                dve.scalar_tensor_tensor(ckv[0:n, c, LAT:CROW], kv[0:n, 0:KVL], rs[0:n, 5 + 2 * c:6 + 2 * c], gkv[0:n, :],
                                         ALU.mult, ALU.mult)
                dve.drain()
                rotate(ckv[0:n, c, 0:16], ckv[0:n, c, 16:32], kv[0:n, KVL:288].rearrange("p (b c) -> p b c", b=2),
                       bc(cos[0:n, c, :], [n, 2, 16], 1), bc(sin[0:n, c, :], [n, 2, 16], 1), [n, 2, 16], 0)
                dve.drain()
                dve.engine_nop().then_inc(S("ckv_done"), 1)
                if i == 0:
                    dve.wait_ge(S("state_T"), 1)
                    for c in range(CC):
                        dve.tensor_copy(seg(c, 0, W - 1), PS[6 + c // 2][:, 256 * (c % 2):256 * (c % 2) + 240]
                                        .rearrange("p (s u) -> p s u", u=W - 1)).then_inc(S("state_ev"), 1)

            def gated(c):
                e, a = eg[:, c % 2, :], PS[6 if c % 2 == 0 else 0]
                dve.wait_ge(S("eg"), c + 1)
                dve.wait_ge(S("proj_done"), 3 + 2 * c + 2)
                tt(glu[:, c, W - 1:SEG0], a[:, 0:SEQ], e[:, 0:SEQ], ALU.mult)
                tt(gpk[:, c, :], a[:, SEQ:T], e[:, SEQ:T], ALU.mult)
                dve.drain()
                dve.tensor_copy(seg(c, W - 1, SEG - 1), gpk[:, c, :].rearrange("p (s q) -> p s q", s=DEC_B)).then_inc(S("glu"), 1)

            def q_rotate(i):
                c = ORDER[i]
                n = CHUNKS[c][1]
                q = qt[c][0:n].rearrange("p (h d) -> p h d", h=H)
                for hb in range(2):
                    dve.wait_ge(S("q_nope"), 2 * i + hb + 1)
                    v = PS[4 + hb][0:n, 0:384].rearrange("p (h d) -> p h d", h=4)[:, :, DN:DQ]
                    v = v.rearrange("p h (b c) -> p h b c", b=2)
                    hs = slice(4 * hb, 4 * hb + 4)
                    cs, sn = (z[0:n, c, :].unsqueeze(1).unsqueeze(1).broadcast_to([n, 4, 2, 16]) for z in (cos, sin))
                    dve.drain()
                    rotate(q[:, hs, DN:DN + 16], q[:, hs, DN + 16:DQ], v, cs, sn, [n, 4, 2, 16], 0)
                dve.drain()
                dve.engine_nop().then_inc(S("q_rope"), 1)

            def q_norm(i):
                c = ORDER[i]
                n = CHUNKS[c][1]
                q = qt[c][0:n].rearrange("p (h d) -> p h d", h=H)
                dve.wait_ge(S("q_sq"), i + 1)
                dve.tensor_reduce(s8[0:n, 0, :], sqs[0:n, 0, :].rearrange("p (h d) -> p h d", h=H), X_AXIS, ALU.add)\
                    .then_inc(S("q_ss"), 1)
                dve.wait_ge(S("q_r"), i + 1)
                tt(q, q, bc(r8[0:n, 0, :], [n, H, DQ], 2), ALU.mult)
                dve.drain()
                if i:
                    tt(q, q, bc(gqk[0:n, :], [n, H, DQ], 1), ALU.mult).then_inc(S("q_done"), 1)
                else:
                    tt(qsn[0:n].rearrange("p (h d) -> p h d", h=H), q[:, :, 0:DN], bc(gqk[0:n, 0:DN], [n, H, DN], 1), ALU.mult)
                    tt(qsr[0:n, 0:256].rearrange("p (h d) -> p h d", h=H), q[:, :, DN:DQ],
                       bc(gqk[0:n, DN:DQ], [n, H, DR], 1), ALU.mult)
                    dve.drain()
                    dve.engine_nop().then_inc(S("q_done"), 1)

            def k_sums(i):
                c = ORDER[i]
                n = CHUNKS[c][1]
                kr = ckv[0:n, c, 0:DR]
                tt(rope_a[0:n, 0:DR], kr, kr, ALU.mult)
                dve.drain()
                dve.tensor_reduce(ss[0:n, 12:13], rope_a[0:n, 0:DR], X_AXIS, ALU.add)
                dve.wait_ge(S("k_sq"), i + 1)
                dve.tensor_reduce(s8[0:n, 1, :], sqs[0:n, 1, 0:512].rearrange("p (h d) -> p h d", h=H), X_AXIS, ALU.add)
                dve.drain()
                ts(s8[0:n, 1, :], s8[0:n, 1, :], ss[0:n, 12:13], None, ALU.add).then_inc(S("k_ss"), 1)

            def k_norm(i):
                c = ORDER[i]
                dve.wait_ge(S("k_r"), i + 1)
                if i:
                    kr = ckv[:, c, 0:DR]
                    k = kt[c].rearrange("p (h d) -> p h d", h=H)
                    tt(k[:, :, 0:DN], PS[(6, 0)[i - 1]][:, :].rearrange("p (h d) -> p h d", h=H), bc(r8[:, 1, :], [128, H, DN], 2), ALU.mult)
                    tt(k[:, :, DN:DQ], bc(kr, [128, H, DR], 1), bc(r8[:, 1, :], [128, H, DR], 2), ALU.mult)
                    dve.drain()
                dve.engine_nop().then_inc(S("k_done"), 1)

            gated(0)
            dve.wait_ge(S("ql_T"), 1)
            dve.tensor_copy(ckvT[:, :, 0:SEQ].rearrange("p l (c x) -> p c l x", c=2),
                            PS[2][:, :].rearrange("p (c l x) -> p c l x", c=2, l=2)).then_inc(S("latT"), 1)
            dve.tensor_copy(ckvT[:, :, SEQ:T], PS[3][:, 0:256].rearrange("p (l x) -> p l x", l=2)[:, :, 0:NS]).then_inc(S("latT"), 1)
            dve.tensor_copy(krn[:], PS[3][:, 256:256 + NS]).then_inc(S("latT"), 1)
            for i, c in enumerate(ORDER):
                r, n = CHUNKS[c]
                dve.wait_ge(S("ql_T"), i + 1)
                src = PS[3][:, 320:512] if c == 2 else PS[4 + c][:, 0:384]
                tt(qlT[:, :, r:r + n], src.rearrange("p (j x) -> p j x", j=3),
                   bc(g_ql[:], [128, 3, n], 2), ALU.mult).then_inc(S("qlT"), 1)
            q_rotate(0)
            gated(1)
            q_norm(0)
            k_sums(0)
            gated(2)
            k_norm(0)
            q_rotate(1)
            q_norm(1)
            dve.wait_ge(S("qs_T"), 1)
            for s2 in range(2):
                ps = slice(64 * s2, 64 * s2 + 64)
                dve.tensor_copy(qsT[ps, :, 64 * s2:64 * s2 + 64], PS[3][ps, 0:256].rearrange("p (a b) -> p a b", a=4))
            dve.tensor_copy(qrT[0:DR, :].rearrange("p (s h q) -> p h s q", s=8, h=8),
                            PS[2][0:DR, :].rearrange("p (h s q) -> p h s q", s=8, h=8))
            dve.drain()
            dve.engine_nop().then_inc(S("qsT"), 1)
            gated(3)
            dve.wait_ge(S("q_abs"), 1)
            for l in range(2):
                dve.tensor_copy(qabs[:, l, :].rearrange("p (s h q) -> p h s q", s=8, h=8),
                                PS[2 + l][:, :].rearrange("p (h s q) -> p h s q", s=8, h=8)).then_inc(S("qabs"), 1)
            k_sums(1)
            dve.wait_ge(S("s_new"), 1)
            tt(snew[0:NS].rearrange("p (s h q) -> p s h q", s=8, h=8), PS[2][0:NS, :].rearrange("p (s h q) -> p s h q", s=8, h=8),
               r8[0:NS, 2, :].unsqueeze(1).unsqueeze(3).broadcast_to([NS, 8, 8, 8]), ALU.mult).then_inc(S("snew"), 1)
            k_norm(1)
            q_rotate(2)
            q_norm(2)
            k_sums(2)
            k_norm(2)
            for b in range(8):
                c, hb, dst = b // 4, b % 2, (kT, qT)[b // 2 % 2]
                dve.wait_ge(S("heads_T"), b + 1)
                dve.tensor_copy(dst[0:DQ, 4 * hb:4 * hb + 4, 128 * c:128 * c + 128],
                                PS[(2, 3, 6, 7)[b % 4]][0:DQ, :].rearrange("p (a b) -> p a b", a=4)).then_inc(S("heads_ev"), 1)

            def scale_half(n, t, half):
                dve.wait_ge(S("rk"), 2 * n + half + 1)
                dve.wait_ge(S("scores"), n * PAGES + 4 * half + 4)
                src = PS[4 + half][:, :].rearrange("p (b c) -> p b c", b=4)[:, :, 64 * t:64 * t + 64]
                tt(s_all[t][:, 4 * half:4 * half + 4, :].rearrange("p b (h q) -> p b h q", h=H),
                   src.rearrange("p b (h q) -> p b h q", h=H),
                   bc(r8[:, 4 * half:4 * half + 4, :], [128, 4, H, DEC_T], 3), ALU.mult).then_inc(S("s_half"), 1)

            def maxima(n, t):
                scale_half(n, t, 1)
                dve.drain()
                dve.tensor_reduce(m1[:, 0:64], s_all[t].rearrange("p b c -> p c b"), X_AXIS, ALU.max)
                dve.drain()
                tt(m1[0:NS, 0:64], m1[0:NS, 0:64], snew[0:NS, bass.ds(n * 64, 64)], ALU.max).then_inc(S("m_part"), 1)

            def diagonal(n):
                dve.wait_ge(S("m_T"), n + 1)
                dve.tensor_reduce(mx[0:64, 0:1], PS[6][0:64, 0:128], X_AXIS, ALU.max)
                dve.drain()
                ts(dg[0:64, 0:64], ident[0:64, 0:64], mx[0:64, 0:1]).then_inc(S("m_diag"), 1)

            def subtract(n, t):
                dve.wait_ge(S("m_all"), n + 1)
                tt(s_all[t], s_all[t], bc(PS[6][:, 128:192], [128, PAGES, 64], 1), ALU.subtract)
                tt(pn[0:NS, :], snew[0:NS, bass.ds(n * 64, 64)], PS[6][0:NS, 128:192], ALU.subtract).then_inc(S("s_sub"), 1)

            def normalise(n):
                dve.wait_ge(S("ck_used"), n + 1)
                dve.reciprocal(rden[0:64, 0:1], PS[7][0:64, 0:1])
                dve.drain()
                ts(ocn[0:64], PS[7][0:64, 4:260], rden[0:64, 0:1]).then_inc(S("oc_n"), 1)

            def keep(n):
                dve.wait_ge(S("oc_T"), n + 1)
                dst = ocT.rearrange("p l (h x) -> p l h x", h=H)[:, :, :, bass.ds(n * DEC_T, DEC_T)]
                dve.tensor_copy(dst, PS[6][:, 256:512].rearrange("p (l x) -> p l x", l=2)[:, :, 0:64].rearrange("p l (h q) -> p l h q", h=H)).then_inc(S("ocT"), 1)

            def taps(j, part):
                for c in (2 * part, 2 * part + 1):
                    w = cw[:, bass.ds(j * CC + c, 1)]
                    dve.scalar_tensor_tensor(acc[:, c, 0:SEQ], glu[:, c, bass.ds(j, SEQ)], w, acc[:, c, 0:SEQ], ALU.mult, ALU.add)

            def sequence(n, t, first, chunk=None):
                for b in range(PAGES):
                    m = n * PAGES + b
                    dve.wait_ge(S("sq"), m + 1)
                    dve.tensor_reduce(s8[:, b, :], sqk[b % 2].rearrange("p (h d) -> p h d", h=H), X_AXIS, ALU.add).then_inc(S("kss"), 1)
                    if b % 4 == 3:
                        half = b // 4
                        if b == 3:
                            dve.wait_ge(S("sqr"), n + 1)
                            dve.tensor_reduce(rss[:], sqr[:], X_AXIS, ALU.add).then_inc(S("rss_done"), 1)
                        dve.drain()
                        h8 = s8[:, 4 * half:4 * half + 4, :]
                        tt(h8, h8, bc(rss[:, 4 * half:4 * half + 4], [128, 4, H], 2), ALU.add).then_inc(S("ss_half"), 1)
                    if b == 5:
                        scale_half(n, t, 0)
                    if not first:
                        if b == 0:
                            maxima(n - 1, 1 - t)
                        if b == 1:
                            diagonal(n - 1)
                        if b == 2:
                            subtract(n - 1, 1 - t)
                        if b == 5:
                            normalise(n - 1)
                        if b == 6:
                            keep(n - 1)
                    taps(4 * n + b // 2, b % 2)
                    if chunk is not None and b == 7:
                        dve.wait_ge(S("s_prod"), chunk + 1)
                        dve.tensor_reduce(acc[:, bass.ds(chunk, 1), SEQ:T].rearrange("p a b -> p (a b)"), s_prod,
                                          X_AXIS, ALU.add).then_inc(S("s_sum"), 1)
                    dve.drain()
            dve.wait_ge(S("snew_m"), 2)
            sequence(0, 0, True, 0)
            with dve.Fori(0, 3) as i:
                sequence(2 * i + 1, 1, False, i + 1)
                sequence(2 * i + 2, 0, False)
            sequence(7, 1, False)
            tt(acc[:, :, SEQ:T], acc[:, :, SEQ:T], bc(g_cb[:], [128, CC, NS], 2), ALU.add).then_inc(S("conv_done"), 1)
            maxima(7, 1)
            diagonal(7)
            subtract(7, 1)
            normalise(7)
            keep(7)

            for c in range(NC):
                dve.wait_ge(S("conv_T"), c + 1)
                dve.drain()
                dve.bn_stats(st6[:], PS[(6, 7, 5)[c]][:, :])
                dve.drain()
                last = dve.bn_aggr(mv[:, c, :], st6[:])
            last.then_inc(S("mv"), 1)

            def p_scores(h):
                dve.wait_ge(S("p_sc"), h + 1)
                if h >= 2:
                    dve.wait_ge(S("p_exp"), h - 1)
                dve.tensor_reduce(pm[:, h % 2, 0:1], PS[h % 2][:, 0:128], X_AXIS, ALU.max)
                dve.tensor_reduce(pm[:, h % 2, 1:2], PS[h % 2][:, 128:384], X_AXIS, ALU.max)
                dve.drain()
                ts(pm[:, h % 2, :], pm[:, h % 2, :], -SCALE).then_inc(S("p_m"), 1)

            def p_rows(h):
                dve.wait_ge(S("p_out"), h + 1)
                dve.reciprocal(rsm[:, h % 2, :], psm[:, h % 2, :])
                dve.drain()
                o = PS[4 + h % 2]
                for c in range(2):
                    last = ts(attn_t[:, c, DV * h:DV * h + DV], o[:, 128 * c:128 * c + DV], rsm[:, h % 2, c:c + 1])
                dve.drain()
                dve.engine_nop().then_inc(S("p_o"), 1)
            for h in range(H + 2):
                if h < H:
                    p_scores(h)
                if h == 0:
                    dve.wait_ge(S("root"), 2)
                    for c in range(NC):
                        ts(conv_t[:, c, :], PS[(6, 7, 5)[c]][:, :], mv[:, c, 0:1], rs[:, 3 + c:4 + c], ALU.subtract, ALU.mult).then_inc(S("ln"), 1)
                if h >= 2:
                    p_rows(h - 2)
                if h == 3:
                    dve.wait_ge(S("attn_s"), 1)
                    dve.tensor_copy(attn_t[0:NS, 2, :], PS[7][0:NS, :]).then_inc(S("attn_rows"), 1)

            def mix(i):
                kind, c = i // 3, i % 3
                r, n = CHUNKS[c]
                dve.wait_ge(S("mix_T"), i + 1)
                k = 4 * kind
                tt(xT[:, k:k + 4, r:r + n], PS[(6, 7, 6, 7, 6, 7)[i]][:, :].rearrange("p (a b) -> p a b", a=4)[:, :, 0:n],
                   bc((g_oa if kind else g_oc)[:], [128, 4, n], 2), ALU.mult).then_inc(S("mixT"), 1)
            dve.engine_nop().then_inc(S("attn_rows"), 1)
            dve.wait_ge(S("root"), 3)
            for c in range(NC):
                ts(conv_t[:, c, :], conv_t[:, c, :], rs[:, 6 + c:7 + c]).then_inc(S("conv_n"), 1)
            for i in range(3):
                mix(i)
            dve.wait_ge(S("root"), 4)
            for c, (r, n) in enumerate(CHUNKS):
                ts(attn_t[0:n, c, :], attn_t[0:n, c, :], rs[0:n, c:c + 1]).then_inc(S("attn_n"), 1)
            for i in range(3, 6):
                mix(i)
            def h_cols(i):
                c = ORDER[i]
                r, n = CHUNKS[c]
                for g in range(2):
                    dve.wait_ge(S("h_T"), 2 * i + g + 1)
                    k = 4 * g
                    tt(xT[:, k:k + 4, r:r + n], PS[(6, 4, 6)[i] + g][:, :].rearrange("p (a b) -> p a b", a=4)[:, :, 0:n],
                       bc(g_ffn[:, k:k + 4], [128, 4, n], 2), ALU.mult).then_inc(S("hT"), 1)
            for i, c in enumerate(ORDER):
                r, n = CHUNKS[c]
                for hf in range(2):
                    dve.wait_ge(S("merged"), 2 * i + hf + 1)
                    xs = X[0:n, c, 512 * hf:512 * hf + 512]
                    tt(xs, xs, PS[(4, 0, 2)[c] + hf][0:n, :], ALU.add)
                dve.drain()
                dve.engine_nop().then_inc(S("h_rows"), 1)
                dve.wait_ge(S("root"), 5 + i)
                ts(xn2[0:n, c, :], X[0:n, c, :], rs[0:n, 9 + c:10 + c]).then_inc(S("xn2"), 1)
                if i == 1:
                    h_cols(0)
            h_cols(1)
            h_cols(2)
            dve.wait_ge(S("route_mm"), 1)
            dve.wait_ge(S("moe_zero"), 1)
            dve.tensor_copy(lgT[:, 0:T], PS[2][0:NE, 0:T]).then_inc(S("lgT"), 1)
            dve.wait_ge(S("route_mm"), 2)
            tt(lg[:], PS[3][:, 0:NC * NE].rearrange("p (c e) -> p c e", c=NC), bc(br[:], [128, NC, NE], 1), ALU.add)
            dve.drain()
            for c in range(NC):
                dve.max(v8[:, c, :], lg[:, c, :])
            dve.drain()
            for c in range(NC):
                dve.max_index(i8[:, c, :], v8[:, c, :], lg[:, c, :])
            tt(gate4[:], v8[:, :, 0:TOPK], v8[:, :, 0:1].broadcast_to([128, NC, TOPK]), ALU.subtract).then_inc(S("gate_d"), 1)
            dve.drain()
            dve.tensor_copy(i8f[:], i8[:])
            dve.drain()
            four = [128, NC, TOPK, NE]
            for c in range(NC):
                tt(eq[:, c], bc(iota[:, 0:NE], [128, TOPK, NE], 1), i8f[:, c, 0:TOPK].unsqueeze(2).broadcast_to([128, TOPK, NE]),
                   ALU.is_equal)
            dve.drain()
            dve.tensor_reduce(M[:], eq.rearrange("p c k e -> p c e k"), X_AXIS, ALU.add)
            dve.drain()
            dve.memset(M[NS:128, 2, :], 0.0)
            dve.drain()
            dve.engine_nop().then_inc(S("routed"), 1)
            dve.wait_ge(S("root"), 8)
            dve.tensor_reduce(gsum[:], gate4[:], X_AXIS, ALU.add)
            dve.drain()
            dve.reciprocal(gsum[:], gsum[:])
            dve.drain()
            tt(gate4[:], gate4[:], bc(gsum[:], [128, NC, TOPK], 2), ALU.mult)
            dve.drain()
            for c in range(NC):
                tt(eq[:, c], eq[:, c], gate4[:, c, :].unsqueeze(2).broadcast_to([128, TOPK, NE]), ALU.mult)
            dve.drain()
            dve.tensor_reduce(G[:], eq.rearrange("p c k e -> p c e k"), X_AXIS, ALU.add)
            dve.wait_ge(S("route_mm"), 3)
            cnt = PS[1][0:NE, 0:128]
            ts(extra[:], cnt, float(SLOTS), None, ALU.is_gt)
            for b in range(2, T // SLOTS):
                dve.drain()
                dve.scalar_tensor_tensor(extra[:], cnt, float(SLOTS * b), extra[:], ALU.is_gt, ALU.add)
            dve.memset(G[NS:128, 2, :], 0.0)
            dve.drain()
            dve.engine_nop().then_inc(S("routed"), 1)
            ts(tmpP[:, 0:OVER // 2], iota[0:NE, 0:OVER // 2], 2.0, 1.0, ALU.mult, ALU.add)
            ts(begun[:, 0:1], pidx[0:NE, :], float(EXTRA_AT), None, ALU.is_equal)
            dve.wait_ge(S("route_mm"), 4)
            dve.scalar_tensor_tensor(lg[:], PS[0][:, 0:NC * NE].rearrange("p (c e) -> p c e", c=NC), BIG, M[:], ALU.add, ALU.mult)
            dve.drain()
            ts(lg[:], lg[:], -BIG, None, ALU.add).then_inc(S("routed"), 1)
            dve.wait_ge(S("route_mm"), 5)
            tt(P[:, 0:OVER // 2], tmpP[:, 0:OVER // 2], PS[4][0:NE, 0:OVER // 2], ALU.is_equal)
            dve.drain()
            dve.tensor_reduce(before[:, 0:1], P[:, 0:OVER // 2], X_AXIS, ALU.add)
            dve.drain()
            tt(before[:, 0:1], before[:, 0:1], begun[:, 0:1], ALU.mult)
            dve.drain()
            ts(extra[:], extra[:], before[:, 0:1], None, ALU.add).then_inc(S("routed"), 1)
            dve.wait_ge(S("route_mm"), 6)
            dve.tensor_copy(posT[:], PS[5][0:NE, 0:384])
            dve.tensor_copy(GT[0:NE, :], PS[6][0:NE, 0:384])
            dve.drain()
            dve.engine_nop().then_inc(S("routed"), 1)
            dve.wait_ge(S("route_mm"), 7)
            dve.scalar_tensor_tensor(before[:], PS[2][0:NE, 0:64], pidx[0:NE, :], iota[0:NE, :], ALU.add, ALU.subtract)
            tt(tab_f[0:1, TAB_ST:TAB_ST + NE], PS[4][0:1, 128:128 + NE], iota[0:1, 0:NE], ALU.add)
            ts(tab_f[0:1, 0:1], PS[4][0:1, 256:257], 0.5, float(NE // 2), ALU.mult, ALU.add)
            dve.drain()
            ts(tmpP[:], before[:], extra[:, 0:1], 0.0, ALU.add, ALU.is_ge)
            ts(begun[:], before[:], 0.0, None, ALU.is_le)
            dve.drain()
            tt(P[:], tmpP[:], begun[:], ALU.mult)
            ts(before[:], before[:], float(SLOTS), BIG, ALU.mult, ALU.add)
            dve.drain()
            tt(tmpP[:], before[:], P[:], ALU.mult).then_inc(S("routed"), 1)
            dve.wait_ge(S("route_mm"), 8)
            ts(tab_f[0:1, TAB_E:TAB_E + 64], PS[6][0:1, 384:448], -1.0, None, ALU.add)
            dve.drain()
            dve.tensor_copy(tab[0:1, 0:TAB_ST + NE], tab_f[0:1, 0:TAB_ST + NE])
            dve.tensor_copy(tab[0:1, TAB_E:TAB_W], tab_f[0:1, TAB_E:TAB_W])
            ts(posI, PS[7][:, 0:384].rearrange("p (c i) -> p c i", c=NC)[:, :, 0:ITEMS], -BIG, None, ALU.add)
            dve.tensor_copy(gateI, PS[3][:, 0:384].rearrange("p (c i) -> p c i", c=NC)[:, :, 0:ITEMS])
            dve.drain()
            dve.engine_nop().then_inc(S("table"), 1)

            gsb_, usb_, sgb_, hsb, hT = gsb

            def select(i):
                for t in range(2):
                    pos = posI[:, :, bass.ds(2 * i + t, 1)].broadcast_to([128, NC, SLOTS])
                    last = tt(sel[:, :, 64 * t:64 * t + 64], bc(iota, [128, NC, SLOTS], 1), pos, ALU.is_equal)
                dve.drain()
                dve.engine_nop().then_inc(S("sel"), 1)

            def select_gates(i):
                for c in range(NC):
                    pos = [posI[:, c, bass.ds(2 * i + t, 1)] for t in range(2)]
                    gat = [gateI[:, c, bass.ds(2 * i + t, 1)] for t in range(2)]
                    for k in range(3):
                        dve.tensor_scalar(selg[:, c, 64 * k:64 * k + 64], iota, pos[k % 2], gat[k % 2], ALU.is_equal, ALU.mult)
                dve.drain()
                dve.engine_nop().then_inc(S("selg"), 1)

            def take_tokens(v):
                dve.wait_ge(S("gathered"), v)
                for j in range(2):
                    tt(xg[:, 4 * j:4 * j + 4, :], PS[5 + j][:, :].rearrange("p (a b) -> p a b", a=4),
                       bc(g_ffn[:, 4 * j:4 * j + 4], [128, 4, 128], 2), ALU.mult)
                dve.drain()
                dve.engine_nop().then_inc(S("xg"), 1)

            def swiglu(i, t):
                dve.wait_ge(S("gu_done"), 2 * i + t + 1)
                ts(gsb_, PS[0][:, :], LIMIT, None, ALU.min).then_inc(S("g_min"), 1)
                ts(usb_, PS[1][:, :], -LIMIT, LIMIT, ALU.max, ALU.min).then_inc(S("gu_ev"), 1)
                dve.drain()
                dve.scalar_tensor_tensor(usb_, usb_, 1.0, gsb_, ALU.add, ALU.mult)
                dve.drain()
                dve.wait_ge(S("sig"), 2 * i + t + 1)
                tt(hsb, usb_, sgb_, ALU.mult).then_inc(S("h"), 1)

            def add_rows(v):
                for q in range(6):
                    dve.wait_ge(S("combined"), 6 * v + q + 1)
                    xs = X[:, q // 2, 512 * (q % 2):512 * (q % 2) + 512]
                    tt(xs, xs, PS[(5, 6, 7, 1, 0, 5)[q]][:, :], ALU.add).then_inc(S("y_add"), 1)

            def add_bias(q):
                dve.wait_ge(S("y_bias"), q + 1)
                xs = X[:, q // 2, 512 * (q % 2):512 * (q % 2) + 512]
                tt(xs, xs, PS[(0, 1, 2, 4, 0, 1)[q]][:, :], ALU.add).then_inc(S("ybias"), 1)

            select(0)
            add_bias(0)
            add_bias(1)
            take_tokens(1)
            for q in range(2, 6):
                add_bias(q)
            dve.engine_nop().then_inc(S("gu_ev"), 1)
            select_gates(0)
            n_iter = dve.value_load(tab[0:1, 0:1], min_val=NE // 2, max_val=MAX_ITER)
            with dve.Fori(0, n_iter) as i:
                dve.wait_ge(S("gathered"), i + 1)
                select(i + 1)
                swiglu(i, 0)
                add_rows(i)
                swiglu(i, 1)
                dve.wait_ge(S("sel_T"), i + 1)
                select_gates(i + 1)
                take_tokens(i + 2)
            add_rows(n_iter)
            dve.drain()
            dve.engine_nop().then_inc(S("y_done"), 1)


_INS = ["x_prompt", "x_sample", "cache_kv_latent", "cache_k_rope", "state_conv", "page_table", "norm_mix", "w_in",
        "norm_q_lat", "w_uq", "norm_kv_lat", "w_ukv", "norm_qk_q", "norm_qk_k", "conv_w", "conv_b", "conv_ln_g",
        "conv_ln_b", "norm_out_conv", "norm_out_attn", "w_out", "norm_ffn", "w_router", "b_router", "w_gate_up",
        "b_gate_up", "w_down", "b_down"]
_OUTS = [(1, SEQ, D), (DEC_B, DEC_T, D), (1, 1, SEQ, KVL), (1, 1, SEQ, DR), (1, 1, W - 1, DC),
         (1, DEC_B, DEC_T, KVL), (1, DEC_B, DEC_T, DR), (1, DEC_B, W - 1, DC)]


def _constants():
    import numpy as np

    f = np.float32
    i = np.arange(128)
    pack = np.zeros((128, C_W), f)
    pack[:, C_ID:C_ID + 128] = np.eye(128, dtype=f)
    pack[:, C_UP:C_UP + 128] = i[:, None] < i[None, :]
    pack[:, C_ONE:C_ONE + 128] = 1
    later = np.where(i[None, :] <= i[:, None], f(0), f(-1e30))
    pack[:, C_CAUS:C_CAUS + 128] = later
    pack[:, C_CAUS + 256:C_CAUS + 384] = later
    pack[:, C_IOTA:C_IOTA + 64] = np.arange(64)
    pack[:, C_PIDX] = i
    pack[:, C_EPS] = EPS
    pack[0, C_ONE0:C_ONE0 + 64] = 1
    pos = np.zeros(NC * 128, f)
    pos[:SEQ] = np.arange(SEQ)
    pos[SEQ:T] = np.tile(PAGE * PAGES + np.arange(DEC_T), DEC_B)
    freq = f(10000.0) ** (-np.arange(16, dtype=f) / f(16))
    ang = pos[:, None] * freq[None, :]
    tabs = [np.ascontiguousarray(t(ang).reshape(NC, 128, 16).transpose(1, 0, 2)).astype(f) for t in (np.cos, np.sin)]
    odd = (np.arange(NE, dtype=np.int32) % 2).reshape(1, NE)
    return {"pack": pack, "cos": tabs[0], "sin": tabs[1], "odd": odd}


def kernel(**inputs):
    import numpy as _np
    import concourse.bacc as _bacc
    from concourse import mybir as _mybir
    from concourse.bass_utils import run_bass_kernel_spmd as _run

    nc = _bacc.Bacc("TRN2", target_bir_lowering=False, num_devices=1)
    arrays, args = {}, []
    for name in _INS:
        a = _np.ascontiguousarray(inputs[name])
        arrays[f"in_{name}_dram"] = a
        args.append(nc.dram_tensor(f"in_{name}_dram", a.shape, _mybir.dt.from_np(a.dtype), kind="ExternalInput").ap())
    consts = []
    for name, a in _constants().items():
        arrays[f"const_{name}_dram"] = a
        consts.append(nc.dram_tensor(f"const_{name}_dram", a.shape, _mybir.dt.from_np(a.dtype), kind="ExternalInput").ap())
    outs = [nc.dram_tensor(f"out_{i}_dram", s, _mybir.dt.float32, kind="ExternalOutput").ap() for i, s in enumerate(_OUTS)]
    decoder_layer(nc, args, consts, outs)
    r = _run(nc, [arrays], core_ids=[0])
    return tuple(r.results[0][f"out_{i}_dram"] for i in range(len(_OUTS)))
```
